# Optimizing a Trainium2 kernel written in Bass

```python
import math
import jax, jax.numpy as jnp
from jax import lax
import numpy as np

D_MODEL = 2048
BATCH = 1
SEQ = 256
DEPTH = 1

CHUNK = 64
SB_HEADS = 8
SB_HEAD_DIM = 128
SB_WIDTH = SB_HEADS * SB_HEAD_DIM
SB_QBLOCK = 128
HG_HEADS = 8
HG_KEY_DIM = 128
HG_VAL_DIM = 128
HG_WIDTH = HG_HEADS * HG_KEY_DIM
HG_VWIDTH = HG_HEADS * HG_VAL_DIM
RMS_EPS = 1e-6
PEER_HEADS = 8
PEER_HALF = 128
PEER_QDIM = 2 * PEER_HALF
N_KEYS = 128
N_EXPERTS = N_KEYS * N_KEYS
PEER_TOPK = 16
PEER_TOKBLOCK = 128
DEEPNORM_ALPHA = (2.0 * DEPTH) ** 0.25
DEEPNORM_BETA = (8.0 * DEPTH) ** -0.25
LN_EPS = 1e-5
IN_SIZES = (SB_WIDTH, SB_WIDTH, SB_WIDTH,
            HG_WIDTH, HG_WIDTH, HG_VWIDTH, HG_VWIDTH,
            D_MODEL, D_MODEL)
IN_OFFSETS = tuple(int(v) for v in np.cumsum(IN_SIZES)[:-1])
D_IN = int(sum(IN_SIZES))

kernel_name = "hybrid_sb_hgrn2_peer_deepnorm_block"

def layer_norm(x, g, b):
    xf = x.astype(jnp.float32)
    mu = jnp.mean(xf, axis=-1, keepdims=True)
    var = jnp.mean(jnp.square(xf - mu), axis=-1, keepdims=True)
    y = (xf - mu) * lax.rsqrt(var + LN_EPS) * g.astype(jnp.float32) + b.astype(jnp.float32)
    return y.astype(x.dtype)

def split_heads(t, n_heads):
    bsz, seq, _ = t.shape
    return t.reshape(bsz, seq, n_heads, -1).transpose(0, 2, 1, 3)

def merge_heads(t):
    bsz, nh, seq, d = t.shape
    return t.transpose(0, 2, 1, 3).reshape(bsz, seq, nh * d)

def stick_breaking_attention(q, k, v):
    seq = q.shape[2]
    scale = 1.0 / math.sqrt(q.shape[-1])
    outs = []
    for blk in range(seq // SB_QBLOCK):
        start = blk * SB_QBLOCK
        end = start + SB_QBLOCK
        z = jnp.einsum('bhqd,bhkd->bhqk', q[:, :, start:end], k[:, :, :end]) * scale
        t_pos = start + jnp.arange(SB_QBLOCK)
        s_pos = jnp.arange(end)
        mask = s_pos[None, :] < t_pos[:, None]
        log_1mb = jnp.where(mask, jax.nn.log_sigmoid(-z), 0.0)
        tail = lax.cumsum(log_1mb, axis=3, reverse=True) - log_1mb
        w = jnp.where(mask, jnp.exp(jax.nn.log_sigmoid(z) + tail), 0.0)
        outs.append(jnp.einsum('bhqk,bhkd->bhqd', w, v[:, :, :end]))
    return jnp.concatenate(outs, axis=2)

def hgrn2_chunk_scan(q, k, log_f, v):
    bsz, nh, seq, dk = q.shape
    dv = v.shape[-1]
    nc = seq // CHUNK

    def to_chunks(t):
        return t.reshape(bsz, nh, nc, CHUNK, t.shape[-1]).transpose(2, 0, 1, 3, 4)

    causal = jnp.tril(jnp.ones((CHUNK, CHUNK), dtype=bool))

    def step(state, inp):
        qc, kc, lfc, vc = inp
        b = jnp.cumsum(lfc, axis=2)
        diff = b[:, :, :, None, :] - b[:, :, None, :, :]
        decay = jnp.exp(jnp.where(causal[:, :, None], diff, -jnp.inf))
        scores = jnp.einsum('bhtd,bhsd,bhtsd->bhts', qc, kc, decay)
        o = (jnp.einsum('bhts,bhse->bhte', scores, vc)
             + jnp.einsum('bhtd,bhde->bhte', qc * jnp.exp(b), state))
        b_last = b[:, :, -1:, :]
        new_state = (jnp.exp(b_last[:, :, 0, :])[..., None] * state
                     + jnp.einsum('bhsd,bhse->bhde', kc * jnp.exp(b_last - b), vc))
        return new_state, o

    init = jnp.zeros((bsz, nh, dk, dv), jnp.float32)
    _, o = lax.scan(step, init, (to_chunks(q), to_chunks(k), to_chunks(log_f), to_chunks(v)))
    return o.transpose(1, 2, 0, 3, 4).reshape(bsz, nh, seq, dv)

def hybrid_mixer(h, w_in, lower_bound, hg_norm_g, w_branch_a, w_branch_b, w_out):
    f32 = jnp.float32
    proj = h @ w_in
    sb_q, sb_k, sb_v, hg_q, hg_f, hg_i, hg_g, gate_a, gate_b = jnp.split(proj, IN_OFFSETS, axis=-1)
    a_out = stick_breaking_attention(split_heads(sb_q, SB_HEADS).astype(f32),
                                     split_heads(sb_k, SB_HEADS).astype(f32),
                                     split_heads(sb_v, SB_HEADS).astype(f32))
    a_out = merge_heads(a_out).astype(h.dtype)
    lb = lower_bound.astype(f32).reshape(HG_HEADS, 1, HG_KEY_DIM)
    fgate = lb + (1.0 - lb) * jax.nn.sigmoid(split_heads(hg_f, HG_HEADS).astype(f32))
    o = hgrn2_chunk_scan(split_heads(hg_q, HG_HEADS).astype(f32), 1.0 - fgate, jnp.log(fgate),
                         split_heads(hg_i, HG_HEADS).astype(f32))
    o = o * lax.rsqrt(jnp.mean(jnp.square(o), axis=-1, keepdims=True) + RMS_EPS)
    b_out = (merge_heads(o) * hg_norm_g.astype(f32)
             * jax.nn.silu(hg_g.astype(f32))).astype(h.dtype)
    merged = jax.nn.sigmoid(gate_a) * (a_out @ w_branch_a) + jax.nn.sigmoid(gate_b) * (b_out @ w_branch_b)
    return merged @ w_out

def peer_ffn(h, w_q, sub_keys, u_tab, v_tab):
    bsz, seq, d = h.shape
    n_tok = bsz * seq
    hf = h.reshape(n_tok, d)
    q = (hf @ w_q).reshape(n_tok, PEER_HEADS, 2, PEER_HALF).astype(jnp.float32)
    half_scores = jnp.einsum('thpd,hpnd->thpn', q, sub_keys.astype(jnp.float32))
    s_top, i_top = lax.top_k(half_scores, PEER_TOPK)
    cand = (s_top[:, :, 0, :, None] + s_top[:, :, 1, None, :]).reshape(n_tok, PEER_HEADS, -1)
    cand_idx = (i_top[:, :, 0, :, None] * N_KEYS + i_top[:, :, 1, None, :]).reshape(n_tok, PEER_HEADS, -1)
    best, pos = lax.top_k(cand, PEER_TOPK)
    expert_idx = jnp.take_along_axis(cand_idx, pos, axis=-1)
    gates = jax.nn.softmax(best, axis=-1).astype(h.dtype)
    n_blk = n_tok // PEER_TOKBLOCK

    def block(args):
        xb, ib, gb = args
        act = jnp.einsum('td,thkd->thk', xb, u_tab[ib])
        w = gb * jax.nn.gelu(act, approximate=False)
        return jnp.einsum('thk,thkd->td', w, v_tab[ib])

    out = lax.map(block, (hf.reshape(n_blk, PEER_TOKBLOCK, d),
                          expert_idx.reshape(n_blk, PEER_TOKBLOCK, PEER_HEADS, PEER_TOPK),
                          gates.reshape(n_blk, PEER_TOKBLOCK, PEER_HEADS, PEER_TOPK)))
    return out.reshape(bsz, seq, d)

def setup_inputs(seed: int = 0) -> dict:
    key = jax.random.key(seed)
    ks = jax.random.split(key, 20)

    def nrm(k, shape, scale):
        return jax.random.normal(k, shape, jnp.float32) * scale

    L = DEPTH
    return {
        "x": nrm(ks[0], (BATCH, SEQ, D_MODEL), 1.0),
        "c": nrm(ks[1], (BATCH, D_MODEL), 1.0),
        "w_ada": nrm(ks[2], (L, D_MODEL, 6 * D_MODEL), 0.5 * D_MODEL ** -0.5),
        "b_ada": nrm(ks[3], (L, 6 * D_MODEL), 0.01),
        "w_in": nrm(ks[4], (L, D_MODEL, D_IN), D_MODEL ** -0.5),
        "hg_lb_logits": nrm(ks[5], (DEPTH + 1, HG_WIDTH), 0.1),
        "hg_norm_g": 1.0 + nrm(ks[6], (L, HG_VWIDTH), 0.02),
        "w_branch_a": nrm(ks[7], (L, SB_WIDTH, D_MODEL), SB_WIDTH ** -0.5),
        "w_branch_b": nrm(ks[8], (L, HG_VWIDTH, D_MODEL), HG_VWIDTH ** -0.5),
        "w_out": nrm(ks[9], (L, D_MODEL, D_MODEL), DEEPNORM_BETA * D_MODEL ** -0.5),
        "ln1_g": 1.0 + nrm(ks[10], (L, D_MODEL), 0.02),
        "ln1_b": nrm(ks[11], (L, D_MODEL), 0.02),
        "peer_wq": nrm(ks[12], (L, D_MODEL, PEER_HEADS * PEER_QDIM), D_MODEL ** -0.5),
        "peer_subkeys": nrm(ks[13], (L, PEER_HEADS, 2, N_KEYS, PEER_HALF), PEER_HALF ** -0.5),
        "peer_u": nrm(ks[14], (L, N_EXPERTS, D_MODEL), D_MODEL ** -0.5),
        "peer_v": nrm(ks[15], (L, N_EXPERTS, D_MODEL), DEEPNORM_BETA),
        "ln2_g": 1.0 + nrm(ks[16], (L, D_MODEL), 0.02),
        "ln2_b": nrm(ks[17], (L, D_MODEL), 0.02),
    }

def reference(x, c, w_ada, b_ada, w_in, hg_lb_logits, hg_norm_g, w_branch_a, w_branch_b, w_out,
              ln1_g, ln1_b, peer_wq, peer_subkeys, peer_u, peer_v, ln2_g, ln2_b):
    lower_bounds = jnp.cumsum(jax.nn.softmax(hg_lb_logits.astype(jnp.float32), axis=0), axis=0)
    cond = jax.nn.silu(c)
    for layer in range(DEPTH):
        mod = cond @ w_ada[layer] + b_ada[layer]
        shift1, scale1, gate1, shift2, scale2, gate2 = [m[:, None, :] for m in jnp.split(mod, 6, axis=-1)]
        h = x * (1.0 + scale1) + shift1
        y = hybrid_mixer(h, w_in[layer], lower_bounds[layer], hg_norm_g[layer],
                         w_branch_a[layer], w_branch_b[layer], w_out[layer])
        x = layer_norm(DEEPNORM_ALPHA * x + (1.0 + gate1) * y, ln1_g[layer], ln1_b[layer])
        h = x * (1.0 + scale2) + shift2
        y = peer_ffn(h, peer_wq[layer], peer_subkeys[layer], peer_u[layer], peer_v[layer])
        x = layer_norm(DEEPNORM_ALPHA * x + (1.0 + gate2) * y, ln2_g[layer], ln2_b[layer])
    return x


_drawn_inputs = setup_inputs


def setup_inputs(seed=0):
    import zlib

    import numpy as np

    out = dict(_drawn_inputs(seed))
    spreads = {}
    factors = {'hg_norm_g': 3.181, 'ln2_g': 2.899, 'ln2_b': 2.826}
    for name, (base, spread) in spreads.items():
        noise = np.random.default_rng([zlib.crc32(name.encode()), seed]).standard_normal(out[name].shape)
        drawn = base * np.exp(spread * noise) if base else spread * noise
        out[name] = __import__('jax').numpy.asarray(drawn.astype(out[name].dtype))
    for name, factor in factors.items():
        out[name] = (out[name] * factor).astype(out[name].dtype)
    return out
```

```python
import math
from contextlib import ExitStack, contextmanager

import numpy as np

import concourse.bass as bass
from concourse import mybir

F32 = mybir.dt.float32
U32 = mybir.dt.uint32
ALU = mybir.AluOpType
ACT = mybir.ActivationFunctionType
AX_X = mybir.AxisListType.X
ds = bass.ds

P = 128
TOKENS = 256
BLOCKS = TOKENS // P
D_MODEL = 2048
KT = D_MODEL // P
HEADS = 8
HEAD_DIM = 128
COLS = 256
PAIRS = HEADS * HEAD_DIM // COLS
CHUNK = KT * COLS
BRANCH_KT = HEADS * HEAD_DIM // P
LEVELS = 7
ADA_COLS = 4096
TOPK = 16
SLOTS = HEADS * TOPK
N_KEYS = 128
GROUP = 8
U_RING = 4
ALPHA = 2.0 ** 0.25
LN_EPS = 1e-5
RMS_EPS = 1e-6
Z_SCALE = 1.0 / math.sqrt(HEAD_DIM)
LOWEST = -3.0e38

ATTN0 = 0
HGRN0 = ATTN0 + 3 * PAIRS
GATE0 = HGRN0 + 4 * PAIRS
GATES = D_MODEL // COLS
OUT0 = GATE0 + 3 * GATES
QUERY0 = OUT0 + D_MODEL // COLS
N_CHUNKS = QUERY0 + D_MODEL // COLS

C_IDENT = 0
C_ONES = C_IDENT + P
C_ZEROS = C_ONES + P
C_LATER = C_ZEROS + P
C_BEFORE = C_LATER + P
C_LEVELS = C_BEFORE + 3 * P
C_IOTA = C_LEVELS + 8 * P
C_END = C_IOTA + TOPK


def constants():
    c = np.zeros((P, C_END), np.float32)
    s, t = np.arange(P)[:, None], np.arange(P)[None, :]
    c[:, C_IDENT:C_ONES] = s == t
    c[:, C_ONES:C_ZEROS] = 1.0
    c[:, C_LATER:C_BEFORE] = s > t
    before = c[:, C_BEFORE:C_LEVELS].reshape(P, 3, P)
    before[:, 0] = s < t
    before[:, 1] = 1.0
    before[:, 2] = s < t
    levels = c[:, C_LEVELS:C_IOTA].reshape(P, 8, P)
    levels[:, 0] = s == t
    for n in range(LEVELS):
        half = 1 << n
        levels[:, n + 1] = (s // (2 * half) == t // (2 * half)) & (s // half % 2 == 0) & (t // half % 2 == 1)
    c[:, C_IOTA:] = np.arange(TOPK)
    return c


class Steps:

    def __init__(self, engine, sem):
        self.engine, self.sem, self.base, self.n = engine, sem, 0, 0

    def step(self, instruction):
        instruction.then_inc(self.sem, 1)
        self.n += 1

    def settle(self):
        self.engine.wait_ge(*self.reached())

    def reached(self):
        return self.sem, self.base + self.n

    def link(self, instruction):
        self.step(instruction)
        self.settle()

    @contextmanager
    def loop(self, count, steps):
        before = self.base + self.n
        with self.engine.Fori(0, count) as i:
            self.base, self.n = i * steps + before, 0
            yield i
            assert self.n == steps, (self.n, steps)
        self.base, self.n = before + count * steps, 0


def block_kernel(nc, consts, x_rows, x_t, cond_cols, ada, ada_bias, weights, lb_logits, norm_gain,
                 ln_rows, subkeys_t, expert_u, expert_v, out):
    with ExitStack() as ctx:
        def sb(name, shape, dt=F32):
            return ctx.enter_context(nc.sbuf_tensor(name, shape, dt))

        def sem(name):
            return ctx.enter_context(nc.semaphore(name))

        arena = sb("arena", [P, 7 * CHUNK])
        ring = [arena[:, s * CHUNK:(s + 1) * CHUNK].rearrange("p (k n) -> p k n", k=KT) for s in range(4)]
        ada_slot = [arena[:, (4 + s) * CHUNK:(5 + s) * CHUNK] for s in range(2)]
        branch_in = arena[:, 6 * CHUNK:7 * CHUNK].rearrange("p (a k t) -> p a k t", a=2, k=BRANCH_KT)
        attn_t, hgrn_t = branch_in[:, 0], branch_in[:, 1]
        h2_t = arena[:, 6 * CHUNK:7 * CHUNK].rearrange("p (k t) -> p k t", k=KT)
        ln_slot = [ada_slot[n].rearrange("p (a n) -> p a n", a=2) for n in range(2)]
        row = D_MODEL
        u_slot = [arena[:, s * row:(s + 1) * row] for s in range(U_RING)]
        v_slot = [arena[:, s * row:(s + 1) * row] for s in (4, 5, 6, 7, 8, 9, 12, 13)]

        buf_a = sb("buf_a", [P, CHUNK])
        h_t = buf_a[:].rearrange("p (k t) -> p k t", k=KT)
        xr = buf_a[:].rearrange("p (b n) -> p b n", b=BLOCKS)
        buf_b = sb("buf_b", [P, CHUNK])
        merged_t = buf_b[:].rearrange("p (k t) -> p k t", k=KT)
        decay = buf_b[:].rearrange("p (l m t) -> p l m t", l=8, m=4)
        h2 = buf_b[:].rearrange("p (b n) -> p b n", b=BLOCKS)
        mod_rows = sb("mod_rows", [P, 4 * D_MODEL])
        gate1, shift2, scale2, gate2 = (mod_rows[:, n * D_MODEL:(n + 1) * D_MODEL] for n in range(4))

        cst = sb("cst", [P, C_END])
        ident, ones, zeros = cst[:, C_IDENT:C_ONES], cst[:, C_ONES:C_ZEROS], cst[:, C_ZEROS:C_LATER]
        later = cst[:, C_LATER:C_BEFORE]
        before = cst[:, C_BEFORE:C_LEVELS]
        level_mask = cst[:, C_LEVELS:C_IOTA]
        iota = cst[:, C_IDENT + C_IOTA:C_END]

        cols = sb("cols", [P, 128])
        cond_in, cond_sig, cond = cols[:, 0:16], cols[:, 16:32], cols[:, 32:48]
        shift1, scale1 = cols[:, 48:64], cols[:, 64:80]
        lb, lb_rest, norm_col = cols[:, 80:88], cols[:, 88:96], cols[:, 96:104]
        rms_eps = cols[:, 120:121]
        logits = cols[:, 104:120].rearrange("p (a h) -> p a h", a=2)
        small = sb("small", [P, 64])
        lb_max, lb_sum = small[:, 0:8], small[:, 8:16]
        sq_sum, rstd = small[:, 16:20], small[:, 20:24]
        ln_stats = small[:, 24:48].rearrange("p (a c) -> p a c", a=4)
        ln_mv, ln_rstd, ln_log = small[:, 48:50], small[:, 50:51], small[:, 51:52]

        WORK = 4932
        work = sb("work", [P, WORK])
        at = [0]

        def part(n):
            at[0] += n
            assert at[0] <= WORK, at[0]
            return work[:, at[0] - n:at[0]]

        q_t = part(512).rearrange("p (h t) -> p h t", h=2)
        k_t = part(512).rearrange("p (h t) -> p h t", h=2)
        v_rows = part(512).rearrange("p (b n) -> p b n", b=BLOCKS)
        a_exp = part(768).rearrange("p (h s) -> p h s", h=2)
        a_pen = part(768).rearrange("p (h s) -> p h s", h=2)
        a_log = part(768).rearrange("p (h s) -> p h s", h=2)
        a_w = part(768).rearrange("p (h s) -> p h s", h=2)
        at[0] = 0
        f_gate, f_key, f_log, f_cum, hq_t = (part(512) for _ in range(5))
        hv_rows = part(512).rearrange("p (b n) -> p b n", b=BLOCKS)
        score_t = part(512).rearrange("p (m t) -> p m t", m=4)
        cross_t = part(256).rearrange("p (h t) -> p h t", h=2)
        masked = part(1024).rearrange("p (l t) -> p l t", l=8)
        g_exp, g_t, o_norm = f_log, f_gate, f_cum.rearrange("p (m t) -> p m t", m=4)
        at[0] = 0
        ga_exp, gb_exp, m_a, m_b = (part(512) for _ in range(4))
        at[0] = 0
        sk = part(2048).rearrange("p (c n) -> p c n", c=2 * HEADS)
        pq_t = [part(512) for _ in range(2)]
        out_term = pq_t[0].rearrange("p (b n) -> p b n", b=BLOCKS)
        rest = part(512).rearrange("p (m n) -> p m n", m=4)
        cand = part(512).rearrange("p (b a c) -> p b a c", b=2, a=TOPK)
        onehot = part(512).rearrange("p (b a c) -> p b a c", b=2, a=TOPK)
        top_v = part(64).rearrange("p (m k) -> p m k", m=4)
        top_if = part(64).rearrange("p (m k) -> p m k", m=4)
        best = part(32).rearrange("p (b k) -> p b k", b=2)
        soft = part(32).rearrange("p (b k) -> p b k", b=2)
        hilo_f = part(64).rearrange("p (b k) -> p b k", b=4)
        expert_f = part(64).rearrange("p (b k) -> p b k", b=4)
        soft_sum = part(2)
        top_i = sb("top_i", [P, 4, TOPK], U32)
        pos = sb("pos", [P, 2, TOPK], U32)
        hilo = sb("hilo", [P, 4, TOPK], U32)
        expert = sb("expert", [P, BLOCKS, SLOTS], U32)
        gates = sb("gates", [P, BLOCKS, SLOTS])
        at[0] = 0
        diag = part(GROUP * P).rearrange("p (s n) -> p s n", s=GROUP)
        act, gel, wgt = (part(GROUP) for _ in range(3))
        now = sb("now", [P, GROUP], U32)

        ps = ctx.enter_context(nc.psum_tensor("ps", [P, 8, 512], F32))

        s_const, s_x, s_cols, s_bias = sem("const_loaded"), sem("x_loaded"), sem("cols_loaded"), sem("bias_loaded")
        loaded = [sem(f"slot{s}_loaded") for s in range(4)]
        used = [sem(f"slot{s}_used") for s in range(4)]
        ada_loaded = [sem(f"ada{s}_loaded") for s in range(2)]
        ada_used = [sem(f"ada{s}_used") for s in range(2)]
        dve_step, act_step = sem("vector_steps"), sem("scalar_steps")
        s_cleared, s_sig, s_cond = sem("sums_cleared"), sem("cond_exp"), sem("cond_ready")
        s_mod, s_modc, s_h = sem("mod_products"), sem("mod_cols_ready"), sem("h_ready")
        s_q, s_k, s_v, s_z, s_log = sem("q_ready"), sem("k_ready"), sem("v_ready"), sem("scores"), sem("log_ready")
        s_pen, s_tail, s_u, s_wexp, s_w = sem("penalty"), sem("tails"), sem("w_log"), sem("w_exp"), sem("w_ready")
        s_pv, s_at = sem("attn_products"), sem("attn_ready")
        s_ef, s_f, s_lf, s_d, s_x2 = sem("f_exp"), sem("f_ready"), sem("f_log_ready"), sem("decay_logs"), sem("decay_exp")
        s_hq, s_hv, s_eg, s_g, s_x3 = sem("hq_ready"), sem("hv_ready"), sem("g_exp"), sem("g_ready"), sem("factors")
        s_lv, s_lvr, s_sc = sem("level_products"), sem("levels_read"), sem("hgrn_scores")
        s_cr, s_crr, s_o, s_rs, s_on, s_tr, s_bt = (sem("cross_products"), sem("cross_ready"), sem("o_products"),
                                                    sem("rstd_ready"), sem("o_normed"), sem("o_transposed"), sem("hgrn_ready"))
        s_ea, s_eb, s_a, s_am, s_bm, s_mm, s_row, s_mg = (sem("ga_exp"), sem("gb_exp"), sem("branch_a"), sem("a_merged"), sem("b_merged"),
                                                sem("mod_row_products"), sem("mod_rows_ready"), sem("merged_ready"))
        s_xr, s_ln, s_sk = sem("x_rows_loaded"), [sem("ln1_loaded"), sem("ln2_loaded")], sem("subkeys_loaded")
        s_y, s_var, s_std = sem("out_added"), sem("ln_var"), sem("ln_rstd")
        s_h2, s_h2p, s_h2t = sem("h2_ready"), sem("h2_transposed"), sem("h2t_ready")
        s_pq, s_ks, s_top, s_sd, s_se, s_ex = (sem("pq_ready"), sem("key_scores"), sem("scores_read"), sem("soft_in"), sem("soft_exp"), sem("experts_ready"))
        s_now = sem("indices_set")
        u_loaded = [sem(f"u{s}_loaded") for s in range(U_RING)]
        u_used = [sem(f"u{s}_used") for s in range(U_RING)]
        v_loaded = [sem(f"v{s}_loaded") for s in range(GROUP)]
        v_used = [sem(f"v{s}_used") for s in range(GROUP)]
        s_gel, s_wgt, s_dg, s_out = sem("gelu_ready"), sem("weights_ready"), sem("diag_ready"), sem("out_stored")

        block = ctx.enter_context(nc.Block())

        def wait_alone(engine, sem, value):
            engine.wait_ge(sem, value)
            engine.nop(nofuse=True)

        F_HGRN = (PAIRS, PAIRS, PAIRS, 0)
        F_GATE = tuple(n + PAIRS for n in F_HGRN)
        F_OUT = tuple(n + m * GATES for n, m in zip(F_GATE, (1, 1, 1, 0)))
        F_QUERY = tuple(n + 2 for n in F_OUT)

        @block.sync
        def _(sp):
            sp.dma_start(cols[:, 0:16], cond_cols).then_inc(s_cols, 16)
            sp.dma_start(logits, lb_logits).then_inc(s_cols, 16)
            sp.dma_start(norm_col, norm_gain).then_inc(s_cols, 16)
            sp.dma_start(cst[:], consts).then_inc(s_const, 16)
            sp.wait_ge(s_cleared, 2)
            sp.dma_start(buf_b[0:1, :], ada_bias[0:1, 0:ADA_COLS]).then_inc(s_bias, 16)
            sp.dma_start(mod_rows[0:1, :], ada_bias[0:1, ADA_COLS:]).then_inc(s_bias, 16)
            sp.dma_start(buf_a[:], x_t).then_inc(s_x, 16)

            def stream(turns, first, slots, filled):
                with sp.Fori(0, turns) as i:
                    for s in slots:
                        sp.wait_ge(used[s], i + filled[s])
                        sp.dma_start(arena[:, s * CHUNK:(s + 1) * CHUNK],
                                     weights[ds((i * len(slots) + first + s) * P, P), :]).then_inc(loaded[s], 16)

            sp.wait_ge(ada_used[1], 6)
            stream(PAIRS, ATTN0, range(3), (0, 0, 0, 0))
            stream(PAIRS, HGRN0, range(4), F_HGRN)
            stream(GATES, GATE0, range(3), F_GATE)
            sp.wait_ge(used[1], F_OUT[1])
            sp.dma_start(xr, x_rows).then_inc(s_xr, 16)
            stream(2, OUT0, range(4), F_OUT)
            for n in range(2):
                sp.wait_ge(ada_used[n], 24)
            for n in range(2):
                sp.dma_start(ln_slot[n], ln_rows[2 * n:2 * n + 2, :].partition_broadcast(P)).then_inc(s_ln[n], 16)
            sp.wait_ge(s_mg, GATES)
            sp.dma_start(sk, subkeys_t).then_inc(s_sk, 16)
            stream(2, QUERY0, range(4), F_QUERY)
            for b in range(BLOCKS):
                sp.wait_ge(s_y, GATES + 1 + b)
                sp.dma_start(out[b * P:(b + 1) * P, :], h2[:, b, :]).then_inc(s_out, 16)
            sp.wait_ge(s_out, 16 * BLOCKS)

        @block.gpsimd
        def _(pool):
            for g in range(3):
                with pool.Fori(0, KT // 2) as i:
                    for s in range(2):
                        pool.wait_ge(ada_used[s], i + g * KT // 2)
                        pool.dma_start(ada_slot[s], ada[ds((i * 2 + s) * P, P), g * ADA_COLS:(g + 1) * ADA_COLS])\
                            .then_inc(ada_loaded[s], 16)

            pool.wait_ge(s_ex, 2 * HEADS)
            for s in range(4):
                pool.wait_ge(used[s], F_QUERY[s] + 2)
            for b in range(BLOCKS):
                turns = SLOTS // GROUP
                with pool.Fori(0, turns) as i:
                    pool.wait_ge(v_loaded[GROUP - 1], (i + b * turns) * 16)
                    pool.tensor_copy(now[:], expert[:, b, ds(i * GROUP, GROUP)]).then_inc(s_now, 1)
                    pool.wait_ge(s_now, i + (b * turns + 1))
                    for e in range(GROUP):
                        s = e % U_RING
                        wait_alone(pool, u_used[s], (i + b * turns) * (GROUP // U_RING) + e // U_RING)
                        pool.indirect_dma_start(u_slot[s], None, expert_u,
                                                bass.IndirectOffsetOnAxis(ap=now[:, e:e + 1], axis=0))\
                            .then_inc(u_loaded[s], 16)
                    for e in range(GROUP):
                        wait_alone(pool, v_used[e], i + b * turns)
                        pool.indirect_dma_start(v_slot[e], None, expert_v,
                                                bass.IndirectOffsetOnAxis(ap=now[:, e:e + 1], axis=0))\
                            .then_inc(v_loaded[e], 16)

        @block.scalar
        def _(act_e):
            me = Steps(act_e, act_step)
            run = nc.scalar.activation
            act_e.wait_ge(s_cols, 48)
            run(cond_sig, cond_in, ACT.Exp, scale=-1.0).then_inc(s_sig, 1)
            act_e.wait_ge(s_cond, 1)
            run(logits, logits, ACT.Exp).then_inc(s_sig, 1)
            act_e.wait_ge(s_modc, 1)
            act_e.wait_ge(s_x, 16)
            for k in range(KT // 2, KT):
                run(h_t[:, k], h_t[:, k], ACT.Identity, bias=shift1[:, k:k + 1], scale=scale1[:, k:k + 1]).then_inc(s_h, 1)

            with me.loop(PAIRS, 2) as i:
                act_e.wait_ge(used[0], i + 1)
                run(q_t, ps[:, 0, :].rearrange("p (h t) -> p h t", h=2), ACT.Copy, scale=Z_SCALE).then_inc(s_q, 1)
                act_e.wait_ge(s_z, i + 1)
                me.link(run(a_exp, ps[:, 3:5, 0:384], ACT.Abs))
                me.link(run(a_exp, a_exp, ACT.Exp, scale=-1.0))
                run(a_log, a_exp, ACT.Ln, bias=1.0).then_inc(s_log, 1)
                act_e.wait_ge(used[2], i + 1)
                run(v_rows, ps[:, 2, :].rearrange("p (b n) -> p b n", b=2), ACT.Copy).then_inc(s_v, 1)
                act_e.wait_ge(s_u, i + 1)
                run(a_w, a_w, ACT.Exp).then_inc(s_wexp, 1)
                act_e.wait_ge(s_pv, i + 1)
                run(attn_t[:, ds(i * 2, 2), :], ps[:, 7, :].rearrange("p (h t) -> p h t", h=2), ACT.Copy).then_inc(s_at, 1)

            with me.loop(PAIRS, 5) as i:
                act_e.wait_ge(used[0], i + (PAIRS + 1))
                act_e.wait_ge(s_bt, i)
                run(f_gate, ps[:, 0, :], ACT.Exp, scale=-1.0).then_inc(s_ef, 1)
                act_e.wait_ge(s_f, i * 2 + 2)
                run(f_log, f_gate, ACT.Ln).then_inc(s_lf, 1)
                act_e.wait_ge(used[1], i + (PAIRS + 1))
                run(hq_t, ps[:, 1, :], ACT.Copy).then_inc(s_hq, 1)
                act_e.wait_ge(s_d, i + 1)
                run(decay[:, 0:4], decay[:, 0:4], ACT.Exp).then_inc(s_x2, 1)
                run(decay[:, 4:8], decay[:, 4:8], ACT.Exp).then_inc(s_x2, 1)
                act_e.wait_ge(used[2], i + (PAIRS + 1))
                run(hv_rows, ps[:, 2, :].rearrange("p (b n) -> p b n", b=2), ACT.Copy).then_inc(s_hv, 1)
                act_e.wait_ge(used[3], i + 1)
                run(g_exp, ps[:, 0, :], ACT.Exp, scale=-1.0).then_inc(s_eg, 1)
                act_e.wait_ge(s_cr, i + 1)
                run(cross_t, ps[:, 1, 0:256].rearrange("p (h t) -> p h t", h=2), ACT.Copy).then_inc(s_crr, 1)
                act_e.wait_ge(s_o, i + 1)
                for m in range(4):
                    me.step(run(masked[:, m], ps[:, 7, m * P:(m + 1) * P], ACT.Square, accum_out=sq_sum[:, m:m + 1]))
                me.settle()
                act_e.wait_ge(s_cleared, 3)
                me.link(run(rstd, sq_sum, ACT.Ln, scale=1.0 / HEAD_DIM, bias=rms_eps))
                run(rstd, rstd, ACT.Exp, scale=-0.5).then_inc(s_rs, 1)

            with me.loop(GATES, 0) as i:
                act_e.wait_ge(used[0], i + (F_GATE[0] + 1))
                act_e.wait_ge(s_am, i)
                run(ga_exp, ps[:, 0, :], ACT.Exp, scale=-1.0).then_inc(s_ea, 1)
                act_e.wait_ge(used[1], i + (F_GATE[1] + 1))
                act_e.wait_ge(s_bm, i)
                run(gb_exp, ps[:, 1, :], ACT.Exp, scale=-1.0).then_inc(s_eb, 1)
                for n in range(2):
                    act_e.wait_ge(s_mm, i * 2 + (n + 1))
                    run(mod_rows[:, ds((i * 2 + n) * 512, 512)], ps[:, 5 + n, :], ACT.Copy).then_inc(s_row, 1)

            def rstd_of_ln(n):
                act_e.wait_ge(s_var, n)
                me.link(run(ln_log, ln_mv[:, 1:2], ACT.Ln))
                run(ln_rstd, ln_log, ACT.Exp, scale=-0.5).then_inc(s_std, 1)

            for b in range(BLOCKS):
                rstd_of_ln(b + 1)
            for b in range(BLOCKS):
                for g in range(4):
                    act_e.wait_ge(s_h2p, b * 4 + g + 1)
                    run(h2_t[:, 4 * g:4 * g + 4, b * P:(b + 1) * P], ps[:, 4 + g, :].rearrange("p (k t) -> p k t", k=4), ACT.Copy)\
                        .then_inc(s_h2t, 1)

            with me.loop(2, 0) as i:
                for s in range(4):
                    act_e.wait_ge(used[s], i + (F_QUERY[s] + 1))
                    run(pq_t[s % 2], ps[:, s % 2, :], ACT.Copy).then_inc(s_pq, 1)
                    act_e.wait_ge(s_sd, i * 4 + (s + 1))
                    run(soft, soft, ACT.Exp).then_inc(s_se, 1)

            for b in range(BLOCKS):
                turns = SLOTS // GROUP
                with me.loop(turns, 0) as i:
                    act_e.wait_ge(u_used[U_RING - 1], i * (GROUP // U_RING) + (b * turns + 1) * (GROUP // U_RING))
                    run(gel, act, ACT.Gelu).then_inc(s_gel, 1)
                    act_e.wait_ge(s_wgt, i + (b * turns + 1))
                    for e in range(GROUP):
                        act_e.wait_ge(v_used[e], i + b * turns)
                        run(diag[:, e], ident, ACT.Copy, scale=wgt[:, e:e + 1]).then_inc(s_dg, 1)
                rstd_of_ln(BLOCKS + b + 1)

        @block.tensor
        def _(pe):
            mm = nc.tensor.matmul

            def project_t(bank, slot, rhs, tiles=KT, first=0):
                for c in range(2):
                    for k in range(tiles):
                        last = mm(ps[:, bank, c * TOKENS:(c + 1) * TOKENS], ring[slot][:, first + k, c * P:(c + 1) * P],
                                  rhs[:, k, :], start=(k == 0), stop=(k == tiles - 1))
                return last

            def project_rows(bank, slot, lhs):
                for b in range(BLOCKS):
                    for k in range(KT):
                        last = mm(ps[:, bank, b * COLS:(b + 1) * COLS], lhs[:, k, b * P:(b + 1) * P],
                                  ring[slot][:, k, :], start=(k == 0), stop=(k == KT - 1))
                return last

            pe.wait_ge(s_const, 16)
            for s in range(2):
                pe.wait_ge(ada_used[s], KT // 2)
            for k in range(2 * KT):
                last = mm(ps[:, 0, k:k + 1], buf_b[:, k * P:(k + 1) * P], ones[:, 0:1], start=True, stop=True)
            last.then_inc(s_mod, 1)
            pe.wait_ge(s_h, KT)

            with pe.Fori(0, PAIRS) as i:
                pe.wait_ge(loaded[0], (i + 1) * 16)
                pe.wait_ge(s_q, i)
                project_t(0, 0, h_t).then_inc(used[0], 1)
                pe.wait_ge(loaded[1], (i + 1) * 16)
                pe.wait_ge(s_k, i)
                project_t(1, 1, h_t).then_inc(used[1], 1)
                pe.wait_ge(s_q, i + 1)
                pe.wait_ge(s_k, i + 1)
                for h in range(2):
                    mm(ps[:, 3 + h, 0:256], k_t[:, h, 0:P], q_t[:, h, :], start=True, stop=True)
                    last = mm(ps[:, 3 + h, 256:384], k_t[:, h, P:2 * P], q_t[:, h, P:2 * P], start=True, stop=True)
                last.then_inc(s_z, 1)
                pe.wait_ge(loaded[2], (i + 1) * 16)
                pe.wait_ge(s_v, i)
                project_rows(2, 2, h_t).then_inc(used[2], 1)
                pe.wait_ge(s_pen, i + 1)
                for h in range(2):
                    mm(ps[:, 5 + h, 0:384], later, a_pen[:, h, :], start=True, stop=False, skip_group_check=True)
                    last = mm(ps[:, 5 + h, P:2 * P], ones, a_pen[:, h, 256:384], start=False, stop=True, skip_group_check=True)
                last.then_inc(s_tail, 1)
                pe.wait_ge(s_v, i + 1)
                pe.wait_ge(s_w, i + 1)
                pe.wait_ge(s_at, i)
                for h in range(2):
                    mm(ps[:, 7, h * 256:(h + 1) * 256], v_rows[:, 0, h * P:(h + 1) * P], a_w[:, h, 0:256],
                       start=True, stop=False, skip_group_check=True)
                    last = mm(ps[:, 7, h * 256 + P:(h + 1) * 256], v_rows[:, 1, h * P:(h + 1) * P], a_w[:, h, 256:384],
                              start=False, stop=True, skip_group_check=True)
                last.then_inc(s_pv, 1)

            pe.wait_ge(s_at, PAIRS)
            with pe.Fori(0, PAIRS) as i:
                pe.wait_ge(loaded[0], i * 16 + (F_HGRN[0] + 1) * 16)
                pe.wait_ge(s_g, i)
                project_t(0, 0, h_t).then_inc(used[0], 1)
                pe.wait_ge(loaded[1], i * 16 + (F_HGRN[1] + 1) * 16)
                pe.wait_ge(s_crr, i)
                project_t(1, 1, h_t).then_inc(used[1], 1)
                pe.wait_ge(loaded[2], i * 16 + (F_HGRN[2] + 1) * 16)
                pe.wait_ge(s_bt, i)
                project_rows(2, 2, h_t).then_inc(used[2], 1)
                pe.wait_ge(loaded[3], (i + 1) * 16)
                pe.wait_ge(s_ef, i + 1)
                project_t(0, 3, h_t).then_inc(used[3], 1)
                pe.wait_ge(s_x3, i + 1)
                pe.wait_ge(s_hq, i + 1)
                for h in range(2):
                    last = mm(ps[:, 1, h * P:(h + 1) * P], decay[:, 0, 2 * h], decay[:, 0, 2 * h + 1], start=True, stop=True)
                last.then_inc(s_cr, 1)
                for m in range(4):
                    bank = 3 + 2 * (m % 2)
                    if m >= 2:
                        pe.wait_ge(s_lvr, i * 4 + (m - 1))
                    mm(ps[:, bank, 0:P], f_key[:, m * P:(m + 1) * P], hq_t[:, m * P:(m + 1) * P], start=True, stop=True)
                    for n in range(1, 8):
                        last = mm(ps[:, bank + n // 4, n % 4 * P:(n % 4 + 1) * P], decay[:, n, m], decay[:, n, m],
                                  start=True, stop=True)
                    last.then_inc(s_lv, 1)
                pe.wait_ge(s_hv, i + 1)
                pe.wait_ge(s_crr, i + 1)
                for m in range(4):
                    h, b = m // 2, m % 2
                    pe.wait_ge(s_sc, i * 4 + (m + 1))
                    last = mm(ps[:, 7, m * P:(m + 1) * P], score_t[:, m], hv_rows[:, b, h * P:(h + 1) * P],
                              start=True, stop=(b == 0))
                    if b:
                        last = mm(ps[:, 7, m * P:(m + 1) * P], cross_t[:, h], hv_rows[:, 0, h * P:(h + 1) * P],
                                  start=False, stop=True)
                last.then_inc(s_o, 1)
                pe.wait_ge(s_on, i + 1)
                for m in range(4):
                    last = nc.tensor.transpose(ps[:, 2, m * P:(m + 1) * P], o_norm[:, m], ident)
                last.then_inc(s_tr, 1)

            pe.wait_ge(s_bt, PAIRS)
            for s in range(2):
                pe.wait_ge(ada_used[s], 3 * KT // 2)
            with pe.Fori(0, GATES) as i:
                pe.wait_ge(loaded[0], i * 16 + (F_GATE[0] + 1) * 16)
                pe.wait_ge(s_ea, i)
                project_t(0, 0, h_t).then_inc(used[0], 1)
                pe.wait_ge(loaded[1], i * 16 + (F_GATE[1] + 1) * 16)
                pe.wait_ge(s_eb, i)
                project_t(1, 1, h_t).then_inc(used[1], 1)
                pe.wait_ge(loaded[2], i * 16 + (F_GATE[2] + 1) * 16)
                pe.wait_ge(s_am, i)
                project_t(2, 2, attn_t, BRANCH_KT).then_inc(s_a, 1)
                pe.wait_ge(s_bm, i)
                project_t(3, 2, hgrn_t, BRANCH_KT, BRANCH_KT).then_inc(used[2], 1)
                pe.wait_ge(s_row, i * 2)
                for n in range(2):
                    mm(ps[:, 5 + n, :], ones, mod_rows[:, ds((i * 2 + n) * 512, 512)], start=True, stop=True).then_inc(s_mm, 1)

            pe.wait_ge(s_mg, GATES)
            with pe.Fori(0, 2) as i:
                for s in range(4):
                    pe.wait_ge(loaded[s], i * 16 + (F_OUT[s] + 1) * 16)
                    pe.wait_ge(s_y, i * 4)
                    project_rows(s, s, merged_t).then_inc(used[s], 1)

            for b in range(BLOCKS):
                pe.wait_ge(s_h2, b + 1)
                for g in range(4):
                    if b:
                        pe.wait_ge(s_h2t, (b - 1) * 4 + g + 1)
                    for k in range(4):
                        last = nc.tensor.transpose(ps[:, 4 + g, k * P:(k + 1) * P], h2[:, b, (4 * g + k) * P:(4 * g + k + 1) * P], ident)
                    last.then_inc(s_h2p, 1)

            pe.wait_ge(s_h2t, 4 * BLOCKS)
            pe.wait_ge(s_sk, 16)
            with pe.Fori(0, 2) as i:
                for s in range(4):
                    pe.wait_ge(loaded[s], i * 16 + (F_QUERY[s] + 1) * 16)
                    project_t(s % 2, s, h2_t).then_inc(used[s], 1)
                    pe.wait_ge(s_pq, i * 4 + (s + 1))
                    if s >= 2:
                        pe.wait_ge(s_top, i * 4 + (s - 1))
                    else:
                        pe.wait_ge(s_top, i * 4)
                    for b in range(BLOCKS):
                        for c in range(2):
                            last = mm(ps[:, 2 + s % 2, (2 * b + c) * P:(2 * b + c + 1) * P],
                                      pq_t[s % 2][:, c * TOKENS + b * P:c * TOKENS + (b + 1) * P],
                                      sk[:, ds((i * 4 + s) * 2 + c, 1), :].rearrange("p a n -> p (a n)"), start=True, stop=True)
                    last.then_inc(s_ks, 1)

            pe.wait_ge(s_top, HEADS)
            for b in range(BLOCKS):
                turns = SLOTS // GROUP
                for n in range(4):
                    mm(ps[:, 4 * b + n, :], zeros, h2[:, 0, n * 512:(n + 1) * 512] if b == 0 else cst[:, 0:512],
                       start=True, stop=False, skip_group_check=True)
                with pe.Fori(0, turns) as i:
                    for e in range(GROUP):
                        pe.wait_ge(s_dg, i * GROUP + (b * turns * GROUP + e + 1))
                        pe.wait_ge(v_loaded[e], i * 16 + (b * turns + 1) * 16)
                        for n in range(4):
                            last = mm(ps[:, 4 * b + n, :], diag[:, e], v_slot[e][:, n * 512:(n + 1) * 512],
                                      start=False, stop=False, skip_group_check=True)
                        last.then_inc(v_used[e], 1)

        @block.vector
        def _(dve):
            me = Steps(dve, dve_step)
            v = nc.vector
            v.memset(buf_b[:], 0.0).then_inc(s_cleared, 1)
            v.memset(mod_rows[:], 0.0).then_inc(s_cleared, 1)
            v.memset(rms_eps, RMS_EPS).then_inc(s_cleared, 1)
            dve.wait_ge(s_cols, 48)
            me.link(v.tensor_tensor(lb_max, logits[:, 0], logits[:, 1], ALU.max))
            me.step(v.tensor_tensor(logits[:, 0], logits[:, 0], lb_max, ALU.subtract))
            v.tensor_tensor(logits[:, 1], logits[:, 1], lb_max, ALU.subtract).then_inc(s_cond, 1)
            dve.wait_ge(s_sig, 1)
            me.link(v.tensor_scalar(cond_sig, cond_sig, 1.0, None, ALU.add))
            me.link(v.reciprocal(cond_sig, cond_sig))
            me.link(v.tensor_tensor(cond, cond_in, cond_sig, ALU.mult))
            dve.wait_ge(s_sig, 2)
            me.link(v.tensor_tensor(lb_sum, logits[:, 0], logits[:, 1], ALU.add))
            me.link(v.reciprocal(lb_sum, lb_sum))
            me.link(v.tensor_tensor(lb, logits[:, 0], lb_sum, ALU.mult))
            me.link(v.tensor_scalar(lb_rest, lb, -1.0, 1.0, ALU.mult, ALU.add))

            def ada_tile(s, sums, k, turn, first=False):
                dve.wait_ge(ada_loaded[s], turn * 16 + 16)
                dve.wait_ge(ada_used[1 - s], turn + s)
                v.scalar_tensor_tensor(out=sums, in0=ada_slot[s], scalar=cond[:, ds(k, 1)], in1=sums,
                                       op0=ALU.mult, op1=ALU.add).then_inc(ada_used[s], 1)

            dve.wait_ge(s_bias, 32)
            with dve.Fori(0, KT // 2) as i:
                for s in range(2):
                    ada_tile(s, buf_b[:], i * 2 + s, i)
            dve.wait_ge(s_mod, 1)
            me.step(v.tensor_copy(shift1, ps[:, 0, 0:KT]))
            v.tensor_scalar(scale1, ps[:, 0, KT:2 * KT], 1.0, None, ALU.add).then_inc(s_modc, 1)
            dve.wait_ge(s_modc, 1)
            dve.wait_ge(s_x, 16)
            for k in range(KT // 2):
                v.tensor_scalar(h_t[:, k], h_t[:, k], scale1[:, k:k + 1], shift1[:, k:k + 1], ALU.mult, ALU.add).then_inc(s_h, 1)

            sums = mod_rows[:, 0:ADA_COLS]
            with me.loop(PAIRS, 1) as i:
                for r in range(2):
                    ada_tile(r, sums, i * 4 + r, i * 2 + KT // 2)
                dve.wait_ge(used[1], i + 1)
                v.tensor_copy(k_t, ps[:, 1, :].rearrange("p (h t) -> p h t", h=2)).then_inc(s_k, 1)
                dve.wait_ge(s_log, i + 1)
                z = ps[:, 3:5, 0:384]
                me.link(v.scalar_tensor_tensor(out=a_exp, in0=z, scalar=0.0, in1=a_log, op0=ALU.max, op1=ALU.add))
                for h in range(2):
                    last = v.scalar_tensor_tensor(out=a_pen[:, h], in0=a_exp[:, h], scalar=-1.0, in1=before, op0=ALU.mult, op1=ALU.mult)
                last.then_inc(s_pen, 1)
                v.tensor_tensor(a_w, z, a_exp, ALU.subtract)
                for r in range(2):
                    ada_tile(r, sums, i * 4 + (r + 2), i * 2 + (KT // 2 + 1))
                dve.wait_ge(s_tail, i + 1)
                v.tensor_tensor(a_w, ps[:, 5:7, 0:384], a_w, ALU.add).then_inc(s_u, 1)
                dve.wait_ge(s_wexp, i + 1)
                for h in range(2):
                    last = v.tensor_tensor(a_w[:, h], a_w[:, h], before, ALU.mult)
                last.then_inc(s_w, 1)

            sums = mod_rows[:, ADA_COLS:2 * ADA_COLS]
            with me.loop(PAIRS, 12) as i:
                dve.wait_ge(s_ef, i + 1)
                me.link(v.tensor_scalar(f_gate, f_gate, 1.0, None, ALU.add))
                me.link(v.reciprocal(f_gate, f_gate))
                for h in range(2):
                    v.tensor_scalar(f_gate[:, h * 256:(h + 1) * 256], f_gate[:, h * 256:(h + 1) * 256],
                                    lb_rest[:, ds(i * 2 + h, 1)], lb[:, ds(i * 2 + h, 1)], ALU.mult, ALU.add).then_inc(s_f, 1)
                dve.wait_ge(s_f, i * 2 + 2)
                me.step(v.tensor_scalar(f_key, f_gate, -1.0, 1.0, ALU.mult, ALU.add))
                dve.wait_ge(s_lf, i + 1)
                for m in range(4):
                    me.step(v.tensor_tensor_scan(f_cum[:, m * P:(m + 1) * P], ones, f_log[:, m * P:(m + 1) * P], 0.0, ALU.mult, ALU.add))
                me.settle()
                cum = f_cum.rearrange("p (h b t) -> p h b t", h=2, b=2)
                far = decay[:, 0].rearrange("p (h b) t -> p h b t", h=2)
                for h in range(2):
                    end = cum[:, h, 0, P - 1:P]
                    v.tensor_scalar(far[:, h, 0], cum[:, h, 0], -1.0, end, ALU.mult, ALU.add)
                    v.tensor_copy(far[:, h, 1], cum[:, h, 1])
                for n in range(LEVELS):
                    half = 1 << n
                    c = f_cum.rearrange("p (g a t) -> p g a t", a=2, t=half)
                    d = decay[:, n + 1].rearrange("p m t -> p (m t)").rearrange("p (g a t) -> p g a t", a=2, t=half)
                    end = c[:, :, 0, half - 1:half].to_broadcast([P, 256 // half, half])
                    v.tensor_tensor(d[:, :, 0], end, c[:, :, 0], ALU.subtract)
                    last = v.tensor_tensor(d[:, :, 1], c[:, :, 1], end, ALU.subtract)
                last.then_inc(s_d, 1)
                for r in range(2):
                    ada_tile(r, sums, i * 4 + r, i * 2 + KT)
                dve.wait_ge(s_x2, i * 2 + 2)
                dve.wait_ge(s_hq, i + 1)
                key, query = (x.rearrange("p (h b t) -> p h b t", h=2, b=2) for x in (f_key, hq_t))
                v.tensor_tensor(far[:, :, 0], far[:, :, 0], key[:, :, 0], ALU.mult)
                v.tensor_tensor(far[:, :, 1], far[:, :, 1], query[:, :, 1], ALU.mult)
                for n in range(LEVELS):
                    half = 1 << n
                    d = decay[:, n + 1].rearrange("p m t -> p (m t)").rearrange("p (g a t) -> p g a t", a=2, t=half)
                    key, query = (x.rearrange("p (g a t) -> p g a t", a=2, t=half) for x in (f_key, hq_t))
                    v.tensor_tensor(d[:, :, 0], d[:, :, 0], key[:, :, 0], ALU.mult)
                    last = v.tensor_tensor(d[:, :, 1], d[:, :, 1], query[:, :, 1], ALU.mult)
                last.then_inc(s_x3, 1)
                for r in range(2):
                    ada_tile(r, sums, i * 4 + (r + 2), i * 2 + (KT + 1))
                dve.wait_ge(s_eg, i + 1)
                me.link(v.tensor_scalar(g_exp, g_exp, 1.0, None, ALU.add))
                me.link(v.reciprocal(g_exp, g_exp))
                for h in range(2):
                    w = slice(h * 256, (h + 1) * 256)
                    last = v.scalar_tensor_tensor(out=g_t[:, w], in0=ps[:, 0, w], scalar=norm_col[:, ds(i * 2 + h, 1)],
                                                  in1=g_exp[:, w], op0=ALU.mult, op1=ALU.mult)
                last.then_inc(s_g, 1)
                for m in range(4):
                    dve.wait_ge(s_lv, i * 4 + (m + 1))
                    dve.wait_ge(s_sc, i * 4 + m)
                    bank = 3 + 2 * (m % 2)
                    v.tensor_tensor(masked.rearrange("p l t -> p (l t)"), ps[:, bank:bank + 2, :].rearrange("p a n -> p (a n)"),
                                    level_mask, ALU.mult).then_inc(s_lvr, 1)
                    dve.wait_ge(s_lvr, i * 4 + (m + 1))
                    v.tensor_reduce(score_t[:, m], masked.rearrange("p l t -> p t l"), AX_X, ALU.add).then_inc(s_sc, 1)
                dve.wait_ge(s_rs, i + 1)
                me.step(v.tensor_scalar(o_norm[:, 0], ps[:, 7, 0:P], rstd[:, 0:1], None, ALU.mult))
                me.step(v.tensor_scalar(o_norm[:, 1], ps[:, 7, P:2 * P], rstd[:, 1:2], None, ALU.mult))
                me.step(v.tensor_scalar(o_norm[:, 2], ps[:, 7, 2 * P:3 * P], rstd[:, 2:3], None, ALU.mult))
                v.tensor_scalar(o_norm[:, 3], ps[:, 7, 3 * P:4 * P], rstd[:, 3:4], None, ALU.mult).then_inc(s_on, 1)
                dve.wait_ge(s_tr, i + 1)
                v.tensor_tensor(hgrn_t[:, ds(i * 2, 2), :], ps[:, 2, :].rearrange("p (h t) -> p h t", h=2),
                                g_t.rearrange("p (h t) -> p h t", h=2), ALU.mult).then_inc(s_bt, 1)

            with me.loop(GATES, 4) as i:
                dve.wait_ge(s_ea, i + 1)
                me.link(v.tensor_scalar(ga_exp, ga_exp, 1.0, None, ALU.add))
                me.link(v.reciprocal(ga_exp, ga_exp))
                dve.wait_ge(s_eb, i + 1)
                me.link(v.tensor_scalar(gb_exp, gb_exp, 1.0, None, ALU.add))
                me.link(v.reciprocal(gb_exp, gb_exp))
                dve.wait_ge(s_a, i + 1)
                dve.wait_ge(s_mg, i)
                v.tensor_tensor(m_a, ps[:, 2, :], ga_exp, ALU.mult).then_inc(s_am, 1)
                dve.wait_ge(used[2], i + (F_GATE[2] + 1))
                v.tensor_tensor(m_b, ps[:, 3, :], gb_exp, ALU.mult).then_inc(s_bm, 1)
                dve.wait_ge(s_am, i + 1)
                dve.wait_ge(s_bm, i + 1)
                v.tensor_tensor(merged_t[:, ds(i * 2, 2), :], m_a.rearrange("p (h t) -> p h t", h=2),
                                m_b.rearrange("p (h t) -> p h t", h=2), ALU.add).then_inc(s_mg, 1)

            dve.wait_ge(s_xr, 16)
            dve.wait_ge(s_row, 16)
            y = out_term
            with me.loop(2, 4) as i:
                for s in range(4):
                    dve.wait_ge(used[s], i + (F_OUT[s] + 1))
                    dve.wait_ge(s_y, i * 4 + s)
                    c = ds((i * 4 + s) * COLS, COLS)
                    g = mod_rows[:, ds((i * 4 + s) * COLS, COLS)]
                    for b in range(BLOCKS):
                        last = v.scalar_tensor_tensor(out=y[:, b], in0=g, scalar=1.0, in1=ps[:, s, b * COLS:(b + 1) * COLS],
                                                      op0=ALU.add, op1=ALU.mult)
                    me.link(last)
                    v.scalar_tensor_tensor(out=xr[:, :, c], in0=xr[:, :, c], scalar=ALPHA, in1=y, op0=ALU.mult, op1=ALU.add)\
                        .then_inc(s_y, 1)
            dve.wait_ge(s_y, GATES)

            def layer_norm(rows, n, var_count):
                for q in range(4):
                    me.step(v.bn_stats(ln_stats[:, q], rows[:, q * 512:(q + 1) * 512]))
                me.settle()
                me.link(v.bn_aggr(ln_mv, ln_stats.rearrange("p a c -> p (a c)")))
                v.tensor_scalar(ln_mv[:, 1:2], ln_mv[:, 1:2], LN_EPS, None, ALU.add).then_inc(s_var, 1)
                dve.wait_ge(s_std, var_count)
                me.link(v.tensor_scalar(rows, rows, ln_mv[:, 0:1], ln_rstd, ALU.subtract, ALU.mult))
                me.link(v.tensor_tensor(rows, rows, ln_slot[n][:, 0], ALU.mult))

            dve.wait_ge(s_ln[0], 16)
            for b in range(BLOCKS):
                layer_norm(xr[:, b], 0, b + 1)
                me.link(v.tensor_tensor(xr[:, b], xr[:, b], ln_slot[0][:, 1], ALU.add))
                me.link(v.scalar_tensor_tensor(out=h2[:, b], in0=scale2, scalar=1.0, in1=xr[:, b], op0=ALU.add, op1=ALU.mult))
                v.tensor_tensor(h2[:, b], h2[:, b], shift2, ALU.add).then_inc(s_h2, 1)

            def top16(values, indices, source, reduced):
                n = range(len(source))
                for j in n:
                    me.step(v.max(values[j][:, 0:8], source[j]))
                wait_alone(dve, *me.reached())
                for j in n:
                    me.step(v.max_index(indices[j][:, 0:8], values[j][:, 0:8], source[j]))
                    me.step(v.match_replace(reduced[j], values[j][:, 0:8], source[j], LOWEST))
                wait_alone(dve, *me.reached())
                for j in n:
                    me.step(v.max(values[j][:, 8:16], reduced[j]))
                wait_alone(dve, *me.reached())
                for j in n:
                    last = v.max_index(indices[j][:, 8:16], values[j][:, 8:16], reduced[j])
                    if j < n[-1]:
                        me.step(last)
                return last

            with me.loop(2, 4 * 50) as i:
                for s in range(4):
                    wait_alone(dve, s_ks, i * 4 + (s + 1))
                    bank = 2 + s % 2
                    top16([top_v[:, m] for m in range(4)], [top_i[:, m] for m in range(4)],
                          [ps[:, bank, m * P:(m + 1) * P] for m in range(4)], [rest[:, m] for m in range(4)]).then_inc(s_top, 1)
                    dve.wait_ge(s_top, i * 4 + (s + 1))
                    me.step(v.tensor_copy(top_if, top_i[:]))
                    for b in range(BLOCKS):
                        me.step(v.tensor_tensor(cand[:, b], top_v[:, 2 * b].unsqueeze(2).to_broadcast([P, TOPK, TOPK]),
                                                top_v[:, 2 * b + 1].unsqueeze(1).to_broadcast([P, TOPK, TOPK]), ALU.add))
                    wait_alone(dve, *me.reached())
                    flat = [cand[:, b].rearrange("p a c -> p (a c)") for b in range(BLOCKS)]
                    spare = [onehot[:, b].rearrange("p a c -> p (a c)") for b in range(BLOCKS)]
                    me.link(top16([best[:, b] for b in range(BLOCKS)], [pos[:, b] for b in range(BLOCKS)], flat, spare))
                    for b in range(BLOCKS):
                        last = v.tensor_scalar(soft[:, b], best[:, b], best[:, b, 0:1], None, ALU.subtract)
                    last.then_inc(s_sd, 1)
                    me.step(v.tensor_scalar(hilo[:, 0:2], pos[:], 4, None, ALU.logical_shift_right))
                    me.link(v.tensor_scalar(hilo[:, 2:4], pos[:], 15, None, ALU.bitwise_and))
                    me.link(v.tensor_copy(hilo_f, hilo[:]))
                    for c in range(2):
                        for b in range(BLOCKS):
                            me.step(v.tensor_tensor(onehot[:, b], hilo_f[:, 2 * c + b].unsqueeze(2).to_broadcast([P, TOPK, TOPK]),
                                                    iota.unsqueeze(1).to_broadcast([P, TOPK, TOPK]), ALU.is_equal))
                        me.settle()
                        for b in range(BLOCKS):
                            me.step(v.tensor_tensor(onehot[:, b], onehot[:, b],
                                                    top_if[:, 2 * b + c].unsqueeze(1).to_broadcast([P, TOPK, TOPK]), ALU.mult))
                        me.settle()
                        for b in range(BLOCKS):
                            me.step(v.tensor_reduce(expert_f[:, 2 * c + b], onehot[:, b], AX_X, ALU.add))
                        me.settle()
                    me.link(v.scalar_tensor_tensor(out=expert_f[:, 0:2], in0=expert_f[:, 0:2], scalar=float(N_KEYS), in1=expert_f[:, 2:4],
                                                   op0=ALU.mult, op1=ALU.add))
                    here = ds((i * 4 + s) * TOPK, TOPK)
                    v.tensor_copy(expert[:, :, here], expert_f[:, 0:2]).then_inc(s_ex, 1)
                    dve.wait_ge(s_se, i * 4 + (s + 1))
                    me.link(v.tensor_reduce(soft_sum, soft, AX_X, ALU.add))
                    me.link(v.reciprocal(soft_sum, soft_sum))
                    v.tensor_tensor(gates[:, :, here], soft, soft_sum.unsqueeze(2).to_broadcast([P, BLOCKS, TOPK]), ALU.mult)\
                        .then_inc(s_ex, 1)

            for b in range(BLOCKS):
                turns = SLOTS // GROUP
                with me.loop(turns, 0) as i:
                    for e in range(GROUP):
                        s = e % U_RING
                        dve.wait_ge(u_loaded[s], i * (16 * GROUP // U_RING) + (b * turns * (GROUP // U_RING) + e // U_RING + 1) * 16)
                        v.tensor_tensor_reduce(out=u_slot[s], in0=u_slot[s], in1=h2[:, b], scale=1.0, scalar=0.0,
                                               op0=ALU.mult, op1=ALU.add, accum_out=act[:, e:e + 1]).then_inc(u_used[s], 1)
                    dve.wait_ge(s_gel, i + (b * turns + 1))
                    v.tensor_tensor(wgt, gel, gates[:, b, ds(i * GROUP, GROUP)], ALU.mult).then_inc(s_wgt, 1)
                for e in range(GROUP):
                    dve.wait_ge(v_used[e], (b + 1) * turns)
                rows = h2[:, b]
                me.link(v.scalar_tensor_tensor(out=rows, in0=gate2, scalar=1.0, in1=ps[:, 4 * b:4 * b + 4, :].rearrange("p a n -> p (a n)"),
                                               op0=ALU.add, op1=ALU.mult))
                me.link(v.scalar_tensor_tensor(out=rows, in0=xr[:, b], scalar=ALPHA, in1=rows, op0=ALU.mult, op1=ALU.add))
                if b == 0:
                    dve.wait_ge(s_ln[1], 16)
                layer_norm(rows, 1, BLOCKS + b + 1)
                v.tensor_tensor(rows, rows, ln_slot[1][:, 1], ALU.add).then_inc(s_y, 1)


def kernel(x, c, w_ada, b_ada, w_in, hg_lb_logits, hg_norm_g, w_branch_a, w_branch_b, w_out,
           ln1_g, ln1_b, peer_wq, peer_subkeys, peer_u, peer_v, ln2_g, ln2_b):
    import concourse.bacc as bacc
    from concourse.bass_utils import run_bass_kernel_spmd

    def f32(a):
        return np.asarray(a)

    def chunked(w):
        rows, n = w.shape
        return w.reshape(rows // P, P, n // COLS, COLS).transpose(2, 1, 0, 3).reshape(n // COLS, P, rows // P * COLS)

    w = chunked(f32(w_in)[0])
    sb_q, sb_k, sb_v, hg_q, hg_f, hg_i, hg_g = (w[n * PAIRS:(n + 1) * PAIRS] for n in range(7))
    gate_a, gate_b = w[7 * PAIRS:7 * PAIRS + GATES], w[7 * PAIRS + GATES:]
    branches = np.concatenate([chunked(f32(w_branch_a)[0]), chunked(f32(w_branch_b)[0])], axis=2)

    def woven(*roles):
        return np.stack(roles, axis=1).reshape(-1, P, CHUNK)

    weights = np.concatenate([woven(sb_q, sb_k, sb_v), woven(hg_f, hg_q, hg_i, hg_g), woven(gate_a, gate_b, branches),
                              chunked(f32(w_out)[0]), chunked(f32(peer_wq)[0])])
    x = f32(x)[0]
    arrays = {
        "consts": constants(),
        "x_rows": x.reshape(BLOCKS, P, D_MODEL).transpose(1, 0, 2),
        "x_t": x.reshape(TOKENS, KT, P).transpose(2, 1, 0).reshape(P, CHUNK),
        "cond_cols": f32(c)[0].reshape(KT, P).T,
        "ada": f32(w_ada)[0],
        "ada_bias": f32(b_ada),
        "weights": weights.reshape(N_CHUNKS * P, CHUNK),
        "lb_logits": f32(hg_lb_logits).reshape(2, HEADS, HEAD_DIM).transpose(2, 0, 1),
        "norm_gain": f32(hg_norm_g)[0].reshape(HEADS, HEAD_DIM).T,
        "ln_rows": np.stack([f32(a)[0] for a in (ln1_g, ln1_b, ln2_g, ln2_b)]),
        "subkeys_t": f32(peer_subkeys)[0].reshape(2 * HEADS, N_KEYS, P).transpose(2, 0, 1),
        "expert_u": f32(peer_u)[0],
        "expert_v": f32(peer_v)[0],
    }
    nc = bacc.Bacc("TRN2", target_bir_lowering=False, num_devices=1)
    arrays = {n: np.ascontiguousarray(a) for n, a in arrays.items()}
    args = [nc.dram_tensor(n, a.shape, F32, kind="ExternalInput").ap() for n, a in arrays.items()]
    out = nc.dram_tensor("out", (TOKENS, D_MODEL), F32, kind="ExternalOutput").ap()
    block_kernel(nc, *args, out)
    r = run_bass_kernel_spmd(nc, [arrays], core_ids=[0])
    return r.results[0]["out"].reshape(1, TOKENS, D_MODEL)
```

```python
import math
from contextlib import ExitStack, contextmanager

import numpy as np

import concourse.bass as bass
from concourse import mybir

F32 = mybir.dt.float32
U32 = mybir.dt.uint32
ALU = mybir.AluOpType
ACT = mybir.ActivationFunctionType
AX_X = mybir.AxisListType.X
ds = bass.ds

P = 128
TOKENS = 256
BLOCKS = TOKENS // P
D_MODEL = 2048
KT = D_MODEL // P
HEADS = 8
HEAD_DIM = 128
COLS = 256
PAIRS = HEADS * HEAD_DIM // COLS
CHUNK = KT * COLS
BRANCH_KT = HEADS * HEAD_DIM // P
LEVELS = 7
ADA_COLS = 4096
TOPK = 16
SLOTS = HEADS * TOPK
N_KEYS = 128
U_RING, V_RING = 4, 8
ALPHA = 2.0 ** 0.25
LN_EPS = 1e-5
RMS_EPS = 1e-6
Z_SCALE = 1.0 / math.sqrt(HEAD_DIM)
LOWEST = -3.0e38

ATTN0 = 0
HGRN0 = ATTN0 + 3 * PAIRS
GATE0 = HGRN0 + 4 * PAIRS
GATES = D_MODEL // COLS
OUT0 = GATE0 + 3 * GATES
QUERY0 = OUT0 + D_MODEL // COLS
N_CHUNKS = QUERY0 + D_MODEL // COLS

C_IDENT = 0
C_ONES = C_IDENT + P
C_LATER = C_ONES + P
C_BEFORE = C_LATER + P
C_LEVELS = C_BEFORE + 3 * P
C_IOTA = C_LEVELS + 8 * P
C_END = C_IOTA + TOPK


def constants():
    c = np.zeros((P, C_END), np.float32)
    s, t = np.arange(P)[:, None], np.arange(P)[None, :]
    c[:, C_IDENT:C_ONES] = s == t
    c[:, C_ONES:C_LATER] = 1.0
    c[:, C_LATER:C_BEFORE] = s > t
    before = c[:, C_BEFORE:C_LEVELS].reshape(P, 3, P)
    before[:, 0] = s < t
    before[:, 1] = 1.0
    before[:, 2] = s < t
    levels = c[:, C_LEVELS:C_IOTA].reshape(P, 8, P)
    levels[:, 0] = s == t
    for n in range(LEVELS):
        half = 1 << n
        levels[:, n + 1] = (s // (2 * half) == t // (2 * half)) & (s // half % 2 == 0) & (t // half % 2 == 1)
    c[:, C_IOTA:] = np.arange(TOPK)
    return c


class Steps:

    def __init__(self, engine, sem):
        self.engine, self.sem, self.base, self.n = engine, sem, 0, 0

    def step(self, instruction):
        instruction.then_inc(self.sem, 1)
        self.n += 1

    def settle(self):
        self.engine.wait_ge(*self.reached())

    def reached(self):
        return self.sem, self.base + self.n

    def link(self, instruction):
        self.step(instruction)
        self.settle()

    @contextmanager
    def loop(self, count, steps):
        before = self.base + self.n
        with self.engine.Fori(0, count) as i:
            self.base, self.n = i * steps + before, 0
            yield i
            assert self.n == steps, (self.n, steps)
        self.base, self.n = before + count * steps, 0


def block_kernel(nc, consts, x_rows, x_t, cond_cols, ada, ada_bias, weights, lb_logits, norm_gain,
                 ln_rows, subkeys_t, expert_u, expert_v, out):
    with ExitStack() as ctx:
        def sb(name, shape, dt=F32):
            return ctx.enter_context(nc.sbuf_tensor(name, shape, dt))

        def sem(name):
            return ctx.enter_context(nc.semaphore(name))

        from_one = []

        def sem1(name):
            from_one.append(sem(name))
            return from_one[-1]

        arena = sb("arena", [P, 7 * CHUNK])
        ring = [arena[:, s * CHUNK:(s + 1) * CHUNK].rearrange("p (k n) -> p k n", k=KT) for s in range(4)]
        ada_slot = [arena[:, (4 + s) * CHUNK:(5 + s) * CHUNK] for s in range(2)]
        branch_in = arena[:, 6 * CHUNK:7 * CHUNK].rearrange("p (a k t) -> p a k t", a=2, k=BRANCH_KT)
        attn_t, hgrn_t = branch_in[:, 0], branch_in[:, 1]
        h2_t = arena[:, 6 * CHUNK:7 * CHUNK].rearrange("p (k t) -> p k t", k=KT)
        ln_slot = [arena[:, c * CHUNK:(c + 1) * CHUNK].rearrange("p (a n) -> p a n", a=2) for c in (4, 6)]
        row = D_MODEL
        u_slot = [arena[:, s * row:(s + 1) * row] for s in (4, 5, 6, 7)]
        v_slot = [arena[:, s * row:(s + 1) * row] for s in (8, 9, 10, 11, 0, 1, 2, 3)]

        buf_a = sb("buf_a", [P, CHUNK])
        h_t = buf_a[:].rearrange("p (k t) -> p k t", k=KT)
        xr = buf_a[:].rearrange("p (b n) -> p b n", b=BLOCKS)
        buf_b = sb("buf_b", [P, CHUNK])
        merged_t = buf_b[:].rearrange("p (k t) -> p k t", k=KT)
        decay = buf_b[:].rearrange("p (l m t) -> p l m t", l=8, m=4)
        h2 = buf_b[:].rearrange("p (b n) -> p b n", b=BLOCKS)
        mod_rows = sb("mod_rows", [P, 4 * D_MODEL])
        gate1, shift2, scale2, gate2 = (mod_rows[:, n * D_MODEL:(n + 1) * D_MODEL] for n in range(4))

        late_scores = gate1.rearrange("p (c n) -> p c n", c=2 * HEADS)

        cst = sb("cst", [P, C_END])
        ident, ones = cst[:, C_IDENT:C_ONES], cst[:, C_ONES:C_LATER]
        later = cst[:, C_LATER:C_BEFORE]
        before = cst[:, C_BEFORE:C_LEVELS]
        level_mask = cst[:, C_LEVELS:C_IOTA]
        iota = cst[:, C_IDENT + C_IOTA:C_END]

        cols = sb("cols", [P, 128])
        cond_in, cond_sig, cond = cols[:, 0:16], cols[:, 16:32], cols[:, 32:48]
        shift1, scale1 = cols[:, 48:64], cols[:, 64:80]
        lb, lb_rest, norm_col = cols[:, 80:88], cols[:, 88:96], cols[:, 96:104]
        rms_eps = cols[:, 120:121]
        logits = cols[:, 104:120].rearrange("p (a h) -> p a h", a=2)
        small = sb("small", [P, 64])
        lb_max, lb_sum = small[:, 0:8], small[:, 8:16]
        sq_sum, rstd = small[:, 16:20], small[:, 20:24]
        ln_stats = small[:, 24:48].rearrange("p (a c) -> p a c", a=4)
        ln_mv = [small[:, 48 + 2 * b:50 + 2 * b] for b in range(BLOCKS)]
        ln_rstd = [small[:, 52 + b:53 + b] for b in range(BLOCKS)]
        ln_log = [small[:, 54 + b:55 + b] for b in range(BLOCKS)]

        WORK = 5332
        work = sb("work", [P, WORK])
        at = [0]

        def part(n):
            at[0] += n
            assert at[0] <= WORK, at[0]
            return work[:, at[0] - n:at[0]]

        q_t = part(512).rearrange("p (h t) -> p h t", h=2)
        k_t = part(512).rearrange("p (h t) -> p h t", h=2)
        v_rows = part(512).rearrange("p (b n) -> p b n", b=BLOCKS)
        a_exp = part(768).rearrange("p (h s) -> p h s", h=2)
        a_pen = part(768).rearrange("p (h s) -> p h s", h=2)
        a_log = part(768).rearrange("p (h s) -> p h s", h=2)
        a_w = part(768).rearrange("p (h s) -> p h s", h=2)
        at[0] = 0
        f_gate, f_key, f_log, f_cum, hq_t = (part(512) for _ in range(5))
        hv_rows = part(512).rearrange("p (b n) -> p b n", b=BLOCKS)
        score_t = part(512).rearrange("p (m t) -> p m t", m=4)
        cross_t = part(256).rearrange("p (h t) -> p h t", h=2)
        masked = part(1024).rearrange("p (l t) -> p l t", l=8)
        g_exp, g_t, o_norm = f_log, f_gate, f_cum.rearrange("p (m t) -> p m t", m=4)
        at[0] = 0
        ga_exp, gb_exp, m_a, m_b = (part(512) for _ in range(4))
        at[0] = 0
        sk = part(2048).rearrange("p (c n) -> p c n", c=2 * HEADS)
        pq_t = [part(512) for _ in range(2)]
        out_term = pq_t[0].rearrange("p (b n) -> p b n", b=BLOCKS)
        rest = part(256).rearrange("p (c n) -> p c n", c=2)
        cand = part(256).rearrange("p (a c) -> p a c", a=TOPK)
        onehot = part(512)
        top_v = part(32).rearrange("p (c k) -> p c k", c=2)
        top_if = part(32).rearrange("p (c k) -> p c k", c=2)
        best, soft = part(TOPK), part(TOPK)
        hilo_f, expert_f = part(32), part(32)
        soft_sum = part(1)
        top_i = sb("top_i", [P, 2, TOPK], U32)
        pos = sb("pos", [P, TOPK], U32)
        hilo = sb("hilo", [P, 2, TOPK], U32)
        expert = sb("expert", [P, BLOCKS, SLOTS], U32)
        gates = sb("gates", [P, BLOCKS, SLOTS])
        late = pq_t[0][:, 0:256].rearrange("p (c n) -> p c n", c=2)
        act, gel, wgt = part(TOPK), part(TOPK), part(TOPK)
        diag = part(V_RING * P).rearrange("p (s n) -> p s n", s=V_RING)
        u_now, v_now = sb("u_now", [P, TOPK], U32), sb("v_now", [P, TOPK], U32)

        ps = ctx.enter_context(nc.psum_tensor("ps", [P, 8, 512], F32))

        s_const, s_x, s_cols = sem("const_loaded"), sem("x_loaded"), sem("cols_loaded")
        s_bias = [sem("bias1_loaded"), sem("bias2_loaded")]
        loaded = [sem(f"slot{s}_loaded") for s in range(4)]
        used = [sem1(f"slot{s}_used") for s in range(4)]
        ada_loaded = [sem(f"ada{s}_loaded") for s in range(2)]
        ada_used = [sem1(f"ada{s}_used") for s in range(2)]
        dve_step, act_step = sem("vector_steps"), sem("scalar_steps")
        s_cleared, s_zero, s_sig, s_cond = sem("sums_cleared"), sem("mod_rows_cleared"), sem("cond_exp"), sem("cond_ready")
        s_mod, s_modc, s_h = sem("mod_products"), sem("mod_cols_ready"), sem("h_ready")
        s_q, s_k, s_v, s_z, s_log = sem1("q_ready"), sem1("k_ready"), sem1("v_ready"), sem("scores"), sem("log_ready")
        s_pen, s_tail, s_u, s_wexp, s_w = sem("penalty"), sem("tails"), sem("w_log"), sem("w_exp"), sem("w_ready")
        s_pv, s_at = sem("attn_products"), sem1("attn_ready")
        s_ef, s_f, s_lf, s_d, s_x2 = sem("f_exp"), sem("f_ready"), sem("f_log_ready"), sem("decay_logs"), sem("decay_exp")
        s_hq, s_hv, s_eg, s_g, s_x3 = sem("hq_ready"), sem("hv_ready"), sem("g_exp"), sem1("g_ready"), sem("factors")
        s_lv, s_lvr, s_sc = sem("level_products"), sem("levels_read"), sem1("hgrn_scores")
        s_cr, s_crr, s_o, s_rs = sem("cross_products"), sem("cross_ready"), sem("o_products"), sem("rstd_ready")
        s_on, s_tr, s_bt = sem("o_normed"), sem("o_transposed"), sem1("hgrn_ready")
        s_ea, s_eb, s_a, s_am, s_bm = sem1("ga_exp"), sem1("gb_exp"), sem("branch_a"), sem1("a_merged"), sem1("b_merged")
        s_mm, s_row, s_mg = sem("mod_row_products"), sem1("mod_rows_ready"), sem1("merged_ready")
        s_xr, s_ln, s_sk = sem("x_rows_loaded"), [sem("ln1_loaded"), sem("ln2_loaded")], sem("subkeys_loaded")
        s_y, s_var, s_std, s_xn, s_fin = sem1("out_added"), sem("ln_var"), sem("ln_rstd"), sem("x_normed"), sem("rows_final")
        s_h2, s_h2p, s_h2t = sem("h2_ready"), sem("h2_transposed"), sem("h2t_ready")
        s_pq, s_ks, s_top, s_late = sem("pq_ready"), sem("key_scores"), sem1("scores_read"), sem1("late_scores_kept")
        s_sd, s_se, s_ex, s_gt = sem("soft_in"), sem("soft_exp"), sem("experts_ready"), sem("gates_ready")
        s_read = sem("late_scores_read")
        s_now = sem("indices_set")
        u_loaded = [sem(f"u{s}_loaded") for s in range(U_RING)]
        u_used = [sem1(f"u{s}_used") for s in range(U_RING)]
        v_loaded = [sem(f"v{s}_loaded") for s in range(V_RING)]
        v_used = [sem1(f"v{s}_used") for s in range(V_RING)]
        s_gel, s_wgt, s_dg, s_out = sem("gelu_ready"), sem("weights_ready"), sem("diag_ready"), sem("out_stored")

        block = ctx.enter_context(nc.Block())

        def wait_alone(engine, sem, value):
            engine.wait_ge(sem, value)
            engine.nop(nofuse=True)

        F_ATTN = (4, 4, 4, 4)
        F_HGRN = tuple(n + m * PAIRS for n, m in zip(F_ATTN, (1, 1, 1, 0)))
        F_GATE = tuple(n + PAIRS for n in F_HGRN)
        F_OUT = tuple(n + m * GATES for n, m in zip(F_GATE, (1, 1, 1, 0)))
        F_QUERY = tuple(n + 2 for n in F_OUT)
        F_END = tuple(n + m * 4 for n, m in zip(F_QUERY, (1, 1, 0, 0)))

        @block.sync
        def _(sp):
            sp.dma_start(cols[:, 0:16], cond_cols).then_inc(s_cols, 16)
            sp.dma_start(logits, lb_logits).then_inc(s_cols, 16)
            sp.dma_start(norm_col, norm_gain).then_inc(s_cols, 16)
            sp.wait_ge(s_cleared, 1)
            sp.dma_start(buf_b[0:1, :], ada_bias[0:1, 0:ADA_COLS]).then_inc(s_bias[0], 16)
            with sp.Fori(0, 4) as i:
                for s in range(4):
                    sp.wait_ge(used[s], 1 + i)
                    sp.dma_start(arena[:, s * CHUNK:(s + 1) * CHUNK], ada[ds((i * 4 + s) * P, P), 0:ADA_COLS])\
                        .then_inc(loaded[s], 16)
            sp.dma_start(cst[:], consts).then_inc(s_const, 16)
            sp.dma_start(buf_a[:], x_t).then_inc(s_x, 16)

            def stream(turns, first, slots, filled):
                with sp.Fori(0, turns) as i:
                    for s in slots:
                        sp.wait_ge(used[s], i + (1 + filled[s]))
                        sp.dma_start(arena[:, s * CHUNK:(s + 1) * CHUNK],
                                     weights[ds((i * len(slots) + first + s) * P, P), :]).then_inc(loaded[s], 16)

            stream(PAIRS, ATTN0, range(3), F_ATTN)
            stream(PAIRS, HGRN0, range(4), F_HGRN)
            stream(GATES, GATE0, range(3), F_GATE)
            sp.wait_ge(used[1], 1 + F_OUT[1])
            sp.dma_start(xr, x_rows).then_inc(s_xr, 16)
            stream(2, OUT0, range(4), F_OUT)
            sp.wait_ge(s_mg, 1 + GATES)
            sp.dma_start(sk, subkeys_t).then_inc(s_sk, 16)
            stream(4, QUERY0, range(2), F_QUERY)
            for s in range(2):
                sp.wait_ge(used[s], 1 + F_END[s])
            sp.dma_start(ln_slot[1], ln_rows[2:4, :].partition_broadcast(P)).then_inc(s_ln[1], 16)
            for b in range(BLOCKS):
                sp.wait_ge(s_fin, 1 + b)
                sp.dma_start(out[b * P:(b + 1) * P, :], h2[:, b, :]).then_inc(s_out, 16)
            sp.wait_ge(s_out, 16 * BLOCKS)

        @block.gpsimd
        def _(pool):
            for x in from_one:
                pool.sem_inc(x, 1)
            nc.gpsimd.memset(mod_rows[:], 0.0).then_inc(s_zero, 1)
            pool.wait_ge(s_zero, 1)
            pool.dma_start(mod_rows[0:1, :], ada_bias[0:1, ADA_COLS:]).then_inc(s_bias[1], 16)
            pool.wait_ge(used[3], 1 + 2)
            for g in range(2):
                with pool.Fori(0, KT // 2) as i:
                    for s in range(2):
                        pool.wait_ge(ada_used[s], i + (1 + g * KT // 2))
                        pool.dma_start(ada_slot[s], ada[ds((i * 2 + s) * P, P), (g + 1) * ADA_COLS:(g + 2) * ADA_COLS])\
                            .then_inc(ada_loaded[s], 16)
            for s in range(2):
                pool.wait_ge(ada_used[s], 1 + KT)
            pool.dma_start(ln_slot[0], ln_rows[0:2, :].partition_broadcast(P)).then_inc(s_ln[0], 16)

            def gather(b, h, heads, first=False):
                def take(indices, ring_loaded, n):
                    if not first:
                        per_head = 16 * TOPK // len(ring_loaded)
                        for x in ring_loaded:
                            wait_alone(pool, x, heads * per_head)
                    pool.tensor_copy(indices[:], expert[:, b, ds(h * TOPK, TOPK)]).then_inc(s_now, 1)
                    wait_alone(pool, s_now, heads * 2 + n)

                take(u_now, u_loaded, 1)
                for e in range(TOPK):
                    s = e % U_RING
                    wait_alone(pool, u_used[s], heads * (TOPK // U_RING) + (1 + e // U_RING))
                    pool.indirect_dma_start(u_slot[s], None, expert_u,
                                            bass.IndirectOffsetOnAxis(ap=u_now[:, e:e + 1], axis=0)).then_inc(u_loaded[s], 16)
                take(v_now, v_loaded, 2)
                for e in range(TOPK):
                    s = e % V_RING
                    if first and e == 4:
                        for n in range(2):
                            pool.wait_ge(used[n], 1 + F_END[n])
                    wait_alone(pool, v_used[s], heads * (TOPK // V_RING) + (1 + e // V_RING))
                    pool.indirect_dma_start(v_slot[s], None, expert_v,
                                            bass.IndirectOffsetOnAxis(ap=v_now[:, e:e + 1], axis=0)).then_inc(v_loaded[s], 16)

            pool.wait_ge(s_ex, 1)
            gather(0, 0, 0, first=True)
            with pool.Fori(0, HEADS - 1) as i:
                pool.wait_ge(s_ex, i + 2)
                gather(0, i + 1, i + 1)
            pool.wait_ge(s_ex, BLOCKS * HEADS)
            with pool.Fori(0, HEADS) as i:
                gather(1, i, i + HEADS)

        @block.scalar
        def _(act_e):
            me = Steps(act_e, act_step)
            run = nc.scalar.activation
            act_e.wait_ge(s_cols, 48)
            run(cond_sig, cond_in, ACT.Exp, scale=-1.0).then_inc(s_sig, 1)
            act_e.wait_ge(s_cond, 1)
            run(logits, logits, ACT.Exp).then_inc(s_sig, 1)
            act_e.wait_ge(s_modc, 1)
            act_e.wait_ge(s_x, 16)
            for k in range(KT // 2, KT):
                run(h_t[:, k], h_t[:, k], ACT.Identity, bias=shift1[:, k:k + 1], scale=scale1[:, k:k + 1]).then_inc(s_h, 1)

            with me.loop(PAIRS, 2) as i:
                act_e.wait_ge(used[0], i + (1 + F_ATTN[0] + 1))
                run(q_t, ps[:, 0, :].rearrange("p (h t) -> p h t", h=2), ACT.Copy, scale=Z_SCALE).then_inc(s_q, 1)
                act_e.wait_ge(s_z, i + 1)
                me.link(run(a_exp, ps[:, 3:5, 0:384], ACT.Abs))
                me.link(run(a_exp, a_exp, ACT.Exp, scale=-1.0))
                run(a_log, a_exp, ACT.Ln, bias=1.0).then_inc(s_log, 1)
                act_e.wait_ge(used[2], i + (1 + F_ATTN[2] + 1))
                run(v_rows, ps[:, 2, :].rearrange("p (b n) -> p b n", b=2), ACT.Copy).then_inc(s_v, 1)
                act_e.wait_ge(s_u, i + 1)
                run(a_w, a_w, ACT.Exp).then_inc(s_wexp, 1)
                act_e.wait_ge(s_pv, i + 1)
                run(attn_t[:, ds(i * 2, 2), :], ps[:, 7, :].rearrange("p (h t) -> p h t", h=2), ACT.Copy).then_inc(s_at, 1)

            with me.loop(PAIRS, 5) as i:
                act_e.wait_ge(used[0], i + (1 + F_HGRN[0] + 1))
                act_e.wait_ge(s_bt, 1 + i)
                run(f_gate, ps[:, 0, :], ACT.Exp, scale=-1.0).then_inc(s_ef, 1)
                act_e.wait_ge(s_f, i * 2 + 2)
                run(f_log, f_gate, ACT.Ln).then_inc(s_lf, 1)
                act_e.wait_ge(used[1], i + (1 + F_HGRN[1] + 1))
                run(hq_t, ps[:, 1, :], ACT.Copy).then_inc(s_hq, 1)
                act_e.wait_ge(s_d, i + 1)
                run(decay[:, 0:4], decay[:, 0:4], ACT.Exp).then_inc(s_x2, 1)
                run(decay[:, 4:8], decay[:, 4:8], ACT.Exp).then_inc(s_x2, 1)
                act_e.wait_ge(used[2], i + (1 + F_HGRN[2] + 1))
                run(hv_rows, ps[:, 2, :].rearrange("p (b n) -> p b n", b=2), ACT.Copy).then_inc(s_hv, 1)
                act_e.wait_ge(s_cr, i + 1)
                run(cross_t, ps[:, 2, 0:256].rearrange("p (h t) -> p h t", h=2), ACT.Copy).then_inc(s_crr, 1)
                act_e.wait_ge(used[3], i + (1 + F_HGRN[3] + 1))
                run(g_exp, ps[:, 7, :], ACT.Exp, scale=-1.0).then_inc(s_eg, 1)
                act_e.wait_ge(s_o, i + 1)
                for m in range(4):
                    me.step(run(masked[:, m], ps[:, 5, m * P:(m + 1) * P], ACT.Square, accum_out=sq_sum[:, m:m + 1]))
                me.settle()
                act_e.wait_ge(s_cleared, 2)
                me.link(run(rstd, sq_sum, ACT.Ln, scale=1.0 / HEAD_DIM, bias=rms_eps))
                run(rstd, rstd, ACT.Exp, scale=-0.5).then_inc(s_rs, 1)

            with me.loop(GATES, 0) as i:
                act_e.wait_ge(used[0], i + (1 + F_GATE[0] + 1))
                act_e.wait_ge(s_am, 1 + i)
                run(ga_exp, ps[:, 0, :], ACT.Exp, scale=-1.0).then_inc(s_ea, 1)
                act_e.wait_ge(used[1], i + (1 + F_GATE[1] + 1))
                act_e.wait_ge(s_bm, 1 + i)
                run(gb_exp, ps[:, 1, :], ACT.Exp, scale=-1.0).then_inc(s_eb, 1)
                for n in range(2):
                    act_e.wait_ge(s_mm, i * 2 + (n + 1))
                    run(mod_rows[:, ds((i * 2 + n) * 512, 512)], ps[:, 5 + n, :], ACT.Copy).then_inc(s_row, 1)

            def rstd_of_ln(b, n):
                act_e.wait_ge(s_var, n)
                me.link(run(ln_log[b], ln_mv[b][:, 1:2], ACT.Ln))
                run(ln_rstd[b], ln_log[b], ACT.Exp, scale=-0.5).then_inc(s_std, 1)

            for b in range(BLOCKS):
                rstd_of_ln(b, b + 1)
                act_e.wait_ge(s_std, b + 1)
                me.link(run(ln_log[b], ln_mv[b][:, 0:1], ACT.Copy, scale=-1.0))
                me.link(run(ln_log[b], ln_log[b], ACT.Copy, scale=ln_rstd[b]))
                run(xr[:, b], xr[:, b], ACT.Identity, bias=ln_log[b], scale=ln_rstd[b]).then_inc(s_xn, 1)
            for b in range(BLOCKS):
                for g in range(4):
                    act_e.wait_ge(s_h2p, b * 4 + g + 1)
                    run(h2_t[:, 4 * g:4 * g + 4, b * P:(b + 1) * P], ps[:, 4 + g, :].rearrange("p (k t) -> p k t", k=4), ACT.Copy)\
                        .then_inc(s_h2t, 1)

            with me.loop(2, 0) as i:
                for s in range(4):
                    act_e.wait_ge(used[s % 2], i * 2 + (1 + F_QUERY[s % 2] + s // 2 + 1))
                    run(pq_t[s % 2], ps[:, s % 2, :], ACT.Copy).then_inc(s_pq, 1)
                    act_e.wait_ge(s_ks, i * 4 + (s + 1))
                    run(late_scores[:, ds((i * 4 + s) * 2, 2), :], ps[:, 4 + s % 2, 0:256].rearrange("p (c n) -> p c n", c=2), ACT.Copy)\
                        .then_inc(s_late, 1)
                    act_e.wait_ge(s_sd, i * 4 + (s + 1))
                    run(soft, soft, ACT.Exp).then_inc(s_se, 1)

            def soft_exp(n):
                act_e.wait_ge(s_sd, n)
                run(soft, soft, ACT.Exp).then_inc(s_se, 1)

            def expert_weights(heads):
                act_e.wait_ge(u_used[U_RING - 1], heads * (TOPK // U_RING) + (1 + TOPK // U_RING))
                run(gel, act, ACT.Gelu).then_inc(s_gel, 1)
                act_e.wait_ge(s_wgt, heads + 1)
                for e in range(TOPK):
                    s = e % V_RING
                    act_e.wait_ge(v_used[s], heads * (TOPK // V_RING) + (1 + e // V_RING))
                    run(diag[:, s], ident, ACT.Copy, scale=wgt[:, e:e + 1]).then_inc(s_dg, 1)

            expert_weights(0)
            with me.loop(HEADS - 1, 0) as i:
                soft_exp(i + (HEADS + 1))
                expert_weights(i + 1)
            soft_exp(2 * HEADS)
            expert_weights(HEADS)
            rstd_of_ln(0, BLOCKS + 1)
            with me.loop(HEADS - 1, 0) as i:
                expert_weights(i + (HEADS + 1))
            rstd_of_ln(1, BLOCKS + 2)

        STEPS_OF_CHOICE = 26
        LEVEL_BANKS = (3, 5, 0, 3)

        @block.tensor
        def _(pe):
            mm = nc.tensor.matmul

            def project_t(bank, slot, rhs, tiles=KT, first=0):
                for c in range(2):
                    for k in range(tiles):
                        last = mm(ps[:, bank, c * TOKENS:(c + 1) * TOKENS], ring[slot][:, first + k, c * P:(c + 1) * P],
                                  rhs[:, k, :], start=(k == 0), stop=(k == tiles - 1))
                return last

            def project_rows(bank, slot, lhs):
                for b in range(BLOCKS):
                    for k in range(KT):
                        last = mm(ps[:, bank, b * COLS:(b + 1) * COLS], lhs[:, k, b * P:(b + 1) * P],
                                  ring[slot][:, k, :], start=(k == 0), stop=(k == KT - 1))
                return last

            pe.wait_ge(s_const, 16)
            pe.wait_ge(used[3], 1 + F_ATTN[3])
            for k in range(2 * KT):
                last = mm(ps[:, 0, k:k + 1], buf_b[:, k * P:(k + 1) * P], ones[:, 0:1], start=True, stop=True)
            last.then_inc(s_mod, 1)
            pe.wait_ge(s_h, KT)

            with pe.Fori(0, PAIRS) as i:
                pe.wait_ge(loaded[0], i * 16 + (F_ATTN[0] + 1) * 16)
                pe.wait_ge(s_q, 1 + i)
                project_t(0, 0, h_t).then_inc(used[0], 1)
                pe.wait_ge(loaded[1], i * 16 + (F_ATTN[1] + 1) * 16)
                pe.wait_ge(s_k, 1 + i)
                project_t(1, 1, h_t).then_inc(used[1], 1)
                pe.wait_ge(s_q, i + 2)
                pe.wait_ge(s_k, i + 2)
                for h in range(2):
                    mm(ps[:, 3 + h, 0:256], k_t[:, h, 0:P], q_t[:, h, :], start=True, stop=True)
                    last = mm(ps[:, 3 + h, 256:384], k_t[:, h, P:2 * P], q_t[:, h, P:2 * P], start=True, stop=True)
                last.then_inc(s_z, 1)
                pe.wait_ge(loaded[2], i * 16 + (F_ATTN[2] + 1) * 16)
                pe.wait_ge(s_v, 1 + i)
                project_rows(2, 2, h_t).then_inc(used[2], 1)
                pe.wait_ge(s_pen, i + 1)
                for h in range(2):
                    mm(ps[:, 5 + h, 0:384], later, a_pen[:, h, :], start=True, stop=False, skip_group_check=True)
                    last = mm(ps[:, 5 + h, P:2 * P], ones, a_pen[:, h, 256:384], start=False, stop=True, skip_group_check=True)
                last.then_inc(s_tail, 1)
                pe.wait_ge(s_v, i + 2)
                pe.wait_ge(s_w, i + 1)
                pe.wait_ge(s_at, 1 + i)
                for h in range(2):
                    mm(ps[:, 7, h * 256:(h + 1) * 256], v_rows[:, 0, h * P:(h + 1) * P], a_w[:, h, 0:256],
                       start=True, stop=False, skip_group_check=True)
                    last = mm(ps[:, 7, h * 256 + P:(h + 1) * 256], v_rows[:, 1, h * P:(h + 1) * P], a_w[:, h, 256:384],
                              start=False, stop=True, skip_group_check=True)
                last.then_inc(s_pv, 1)

            pe.wait_ge(s_at, 1 + PAIRS)
            with pe.Fori(0, PAIRS) as i:
                pe.wait_ge(loaded[0], i * 16 + (F_HGRN[0] + 1) * 16)
                project_t(0, 0, h_t).then_inc(used[0], 1)
                pe.wait_ge(loaded[1], i * 16 + (F_HGRN[1] + 1) * 16)
                project_t(1, 1, h_t).then_inc(used[1], 1)
                pe.wait_ge(loaded[2], i * 16 + (F_HGRN[2] + 1) * 16)
                project_rows(2, 2, h_t).then_inc(used[2], 1)
                pe.wait_ge(s_x3, i + 1)
                pe.wait_ge(s_hv, i + 1)
                for h in range(2):
                    last = mm(ps[:, 2, h * P:(h + 1) * P], decay[:, 0, 2 * h], decay[:, 0, 2 * h + 1], start=True, stop=True)
                last.then_inc(s_cr, 1)
                for m in range(4):
                    bank = LEVEL_BANKS[m]
                    if m == 3:
                        pe.wait_ge(s_lvr, i * 4 + 1)
                    mm(ps[:, bank, 0:P], f_key[:, m * P:(m + 1) * P], hq_t[:, m * P:(m + 1) * P], start=True, stop=True)
                    for n in range(1, 8):
                        last = mm(ps[:, bank + n // 4, n % 4 * P:(n % 4 + 1) * P], decay[:, n, m], decay[:, n, m],
                                  start=True, stop=True)
                    last.then_inc(s_lv, 1)
                pe.wait_ge(loaded[3], i * 16 + (F_HGRN[3] + 1) * 16)
                project_t(7, 3, h_t).then_inc(used[3], 1)
                pe.wait_ge(s_crr, i + 1)
                pe.wait_ge(s_lvr, i * 4 + 2)
                for m in range(4):
                    h, b = m // 2, m % 2
                    pe.wait_ge(s_sc, i * 4 + (m + 2))
                    last = mm(ps[:, 5, m * P:(m + 1) * P], score_t[:, m], hv_rows[:, b, h * P:(h + 1) * P],
                              start=True, stop=(b == 0))
                    if b:
                        last = mm(ps[:, 5, m * P:(m + 1) * P], cross_t[:, h], hv_rows[:, 0, h * P:(h + 1) * P],
                                  start=False, stop=True)
                last.then_inc(s_o, 1)
                pe.wait_ge(s_on, i + 1)
                for m in range(4):
                    last = nc.tensor.transpose(ps[:, 6, m * P:(m + 1) * P], o_norm[:, m], ident)
                last.then_inc(s_tr, 1)

            pe.wait_ge(s_bt, 1 + PAIRS)
            for s in range(2):
                pe.wait_ge(ada_used[s], 1 + KT)
            with pe.Fori(0, GATES) as i:
                pe.wait_ge(loaded[0], i * 16 + (F_GATE[0] + 1) * 16)
                pe.wait_ge(s_ea, 1 + i)
                project_t(0, 0, h_t).then_inc(used[0], 1)
                pe.wait_ge(loaded[1], i * 16 + (F_GATE[1] + 1) * 16)
                pe.wait_ge(s_eb, 1 + i)
                project_t(1, 1, h_t).then_inc(used[1], 1)
                pe.wait_ge(loaded[2], i * 16 + (F_GATE[2] + 1) * 16)
                pe.wait_ge(s_am, 1 + i)
                project_t(2, 2, attn_t, BRANCH_KT).then_inc(s_a, 1)
                pe.wait_ge(s_bm, 1 + i)
                project_t(3, 2, hgrn_t, BRANCH_KT, BRANCH_KT).then_inc(used[2], 1)
                pe.wait_ge(s_row, i * 2 + 1)
                for n in range(2):
                    mm(ps[:, 5 + n, :], ones, mod_rows[:, ds((i * 2 + n) * 512, 512)], start=True, stop=True).then_inc(s_mm, 1)

            pe.wait_ge(s_mg, 1 + GATES)
            with pe.Fori(0, 2) as i:
                for s in range(4):
                    pe.wait_ge(loaded[s], i * 16 + (F_OUT[s] + 1) * 16)
                    pe.wait_ge(s_y, i * 4 + 1)
                    project_rows(s, s, merged_t).then_inc(used[s], 1)

            for b in range(BLOCKS):
                pe.wait_ge(s_h2, b + 1)
                for g in range(4):
                    if b:
                        pe.wait_ge(s_h2t, (b - 1) * 4 + g + 1)
                    for k in range(4):
                        last = nc.tensor.transpose(ps[:, 4 + g, k * P:(k + 1) * P], h2[:, b, (4 * g + k) * P:(4 * g + k + 1) * P], ident)
                    last.then_inc(s_h2p, 1)

            pe.wait_ge(s_h2t, 4 * BLOCKS)
            pe.wait_ge(s_sk, 16)
            with pe.Fori(0, 2) as i:
                for s in range(4):
                    pe.wait_ge(loaded[s % 2], i * 32 + (F_QUERY[s % 2] + s // 2 + 1) * 16)
                    project_t(s % 2, s % 2, h2_t).then_inc(used[s % 2], 1)
                    pe.wait_ge(s_pq, i * 4 + (s + 1))
                    pe.wait_ge(s_top, i * 4 + (1 + max(s - 1, 0)))
                    pe.wait_ge(s_late, i * 4 + (1 + max(s - 1, 0)))
                    for b in range(BLOCKS):
                        for c in range(2):
                            last = mm(ps[:, 2 + 2 * b + s % 2, c * P:(c + 1) * P],
                                      pq_t[s % 2][:, c * TOKENS + b * P:c * TOKENS + (b + 1) * P],
                                      sk[:, ds((i * 4 + s) * 2 + c, 1), :].rearrange("p a n -> p (a n)"), start=True, stop=True)
                    last.then_inc(s_ks, 1)

            def weigh_rows(b, heads, first=False):
                for e in range(TOPK):
                    s = e % V_RING
                    pe.wait_ge(s_dg, heads * TOPK + (e + 1))
                    pe.wait_ge(v_loaded[s], heads * (16 * TOPK // V_RING) + (e // V_RING + 1) * 16)
                    for n in range(4):
                        last = mm(ps[:, 4 * b + n, :], diag[:, s], v_slot[s][:, n * 512:(n + 1) * 512],
                                  start=first and e == 0, stop=False, skip_group_check=True)
                    last.then_inc(v_used[s], 1)

            pe.wait_ge(s_top, 1 + HEADS)
            pe.wait_ge(s_late, 1 + HEADS)
            for b in range(BLOCKS):
                weigh_rows(b, b * HEADS, first=True)
                with pe.Fori(0, HEADS - 1) as i:
                    weigh_rows(b, i + (b * HEADS + 1))

        @block.vector
        def _(dve):
            me = Steps(dve, dve_step)
            v = nc.vector
            v.memset(buf_b[:], 0.0).then_inc(s_cleared, 1)
            v.memset(rms_eps, RMS_EPS).then_inc(s_cleared, 1)
            dve.wait_ge(s_cols, 48)
            me.link(v.tensor_tensor(lb_max, logits[:, 0], logits[:, 1], ALU.max))
            me.step(v.tensor_tensor(logits[:, 0], logits[:, 0], lb_max, ALU.subtract))
            v.tensor_tensor(logits[:, 1], logits[:, 1], lb_max, ALU.subtract).then_inc(s_cond, 1)
            dve.wait_ge(s_sig, 1)
            me.link(v.tensor_scalar(cond_sig, cond_sig, 1.0, None, ALU.add))
            me.link(v.reciprocal(cond_sig, cond_sig))
            me.link(v.tensor_tensor(cond, cond_in, cond_sig, ALU.mult))
            dve.wait_ge(s_sig, 2)
            me.link(v.tensor_tensor(lb_sum, logits[:, 0], logits[:, 1], ALU.add))
            me.link(v.reciprocal(lb_sum, lb_sum))
            me.link(v.tensor_tensor(lb, logits[:, 0], lb_sum, ALU.mult))
            me.link(v.tensor_scalar(lb_rest, lb, -1.0, 1.0, ALU.mult, ALU.add))

            def ada_tile(s, sums, k, turn):
                dve.wait_ge(ada_loaded[s], turn * 16 + 16)
                dve.wait_ge(ada_used[1 - s], turn + (1 + s))
                v.scalar_tensor_tensor(out=sums, in0=ada_slot[s], scalar=cond[:, ds(k, 1)], in1=sums,
                                       op0=ALU.mult, op1=ALU.add).then_inc(ada_used[s], 1)

            dve.wait_ge(s_bias[0], 16)
            with dve.Fori(0, 4) as i:
                for s in range(4):
                    dve.wait_ge(loaded[s], i * 16 + 16)
                    dve.wait_ge(used[s - 1], i + (1 + (s > 0)))
                    v.scalar_tensor_tensor(out=buf_b[:], in0=arena[:, s * CHUNK:(s + 1) * CHUNK], scalar=cond[:, ds(i * 4 + s, 1)],
                                           in1=buf_b[:], op0=ALU.mult, op1=ALU.add).then_inc(used[s], 1)
            dve.wait_ge(s_mod, 1)
            me.step(v.tensor_copy(shift1, ps[:, 0, 0:KT]))
            v.tensor_scalar(scale1, ps[:, 0, KT:2 * KT], 1.0, None, ALU.add).then_inc(s_modc, 1)
            dve.wait_ge(s_modc, 1)
            dve.wait_ge(s_x, 16)
            for k in range(KT // 2):
                v.tensor_scalar(h_t[:, k], h_t[:, k], scale1[:, k:k + 1], shift1[:, k:k + 1], ALU.mult, ALU.add).then_inc(s_h, 1)

            dve.wait_ge(s_bias[1], 16)
            sums = mod_rows[:, 0:ADA_COLS]
            with me.loop(PAIRS, 1) as i:
                for r in range(2):
                    ada_tile(r, sums, i * 4 + r, i * 2)
                dve.wait_ge(used[1], i + (1 + F_ATTN[1] + 1))
                v.tensor_copy(k_t, ps[:, 1, :].rearrange("p (h t) -> p h t", h=2)).then_inc(s_k, 1)
                dve.wait_ge(s_log, i + 1)
                z = ps[:, 3:5, 0:384]
                me.link(v.scalar_tensor_tensor(out=a_exp, in0=z, scalar=0.0, in1=a_log, op0=ALU.max, op1=ALU.add))
                for h in range(2):
                    last = v.scalar_tensor_tensor(out=a_pen[:, h], in0=a_exp[:, h], scalar=-1.0, in1=before, op0=ALU.mult, op1=ALU.mult)
                last.then_inc(s_pen, 1)
                v.tensor_tensor(a_w, z, a_exp, ALU.subtract)
                for r in range(2):
                    ada_tile(r, sums, i * 4 + (r + 2), i * 2 + 1)
                dve.wait_ge(s_tail, i + 1)
                v.tensor_tensor(a_w, ps[:, 5:7, 0:384], a_w, ALU.add).then_inc(s_u, 1)
                dve.wait_ge(s_wexp, i + 1)
                for h in range(2):
                    last = v.tensor_tensor(a_w[:, h], a_w[:, h], before, ALU.mult)
                last.then_inc(s_w, 1)

            sums = mod_rows[:, ADA_COLS:2 * ADA_COLS]
            with me.loop(PAIRS, 9) as i:
                dve.wait_ge(s_ef, i + 1)
                me.link(v.tensor_scalar(f_gate, f_gate, 1.0, None, ALU.add))
                me.link(v.reciprocal(f_gate, f_gate))
                for h in range(2):
                    v.tensor_scalar(f_gate[:, h * 256:(h + 1) * 256], f_gate[:, h * 256:(h + 1) * 256],
                                    lb_rest[:, ds(i * 2 + h, 1)], lb[:, ds(i * 2 + h, 1)], ALU.mult, ALU.add).then_inc(s_f, 1)
                dve.wait_ge(s_f, i * 2 + 2)
                me.step(v.tensor_scalar(f_key, f_gate, -1.0, 1.0, ALU.mult, ALU.add))
                dve.wait_ge(s_lf, i + 1)
                for m in range(4):
                    me.step(v.tensor_tensor_scan(f_cum[:, m * P:(m + 1) * P], ones, f_log[:, m * P:(m + 1) * P], 0.0, ALU.mult, ALU.add))
                me.settle()
                cum = f_cum.rearrange("p (h b t) -> p h b t", h=2, b=2)
                far = decay[:, 0].rearrange("p (h b) t -> p h b t", h=2)
                for h in range(2):
                    end = cum[:, h, 0, P - 1:P]
                    v.tensor_scalar(far[:, h, 0], cum[:, h, 0], -1.0, end, ALU.mult, ALU.add)
                    v.tensor_copy(far[:, h, 1], cum[:, h, 1])
                for n in range(LEVELS):
                    half = 1 << n
                    c = f_cum.rearrange("p (g a t) -> p g a t", a=2, t=half)
                    d = decay[:, n + 1].rearrange("p m t -> p (m t)").rearrange("p (g a t) -> p g a t", a=2, t=half)
                    end = c[:, :, 0, half - 1:half].to_broadcast([P, 256 // half, half])
                    v.tensor_tensor(d[:, :, 0], end, c[:, :, 0], ALU.subtract)
                    last = v.tensor_tensor(d[:, :, 1], c[:, :, 1], end, ALU.subtract)
                last.then_inc(s_d, 1)
                for r in range(2):
                    ada_tile(r, sums, i * 4 + r, i * 2 + KT // 2)
                dve.wait_ge(s_x2, i * 2 + 2)
                dve.wait_ge(s_hq, i + 1)
                key, query = (x.rearrange("p (h b t) -> p h b t", h=2, b=2) for x in (f_key, hq_t))
                v.tensor_tensor(far[:, :, 0], far[:, :, 0], key[:, :, 0], ALU.mult)
                v.tensor_tensor(far[:, :, 1], far[:, :, 1], query[:, :, 1], ALU.mult)
                for n in range(LEVELS):
                    half = 1 << n
                    d = decay[:, n + 1].rearrange("p m t -> p (m t)").rearrange("p (g a t) -> p g a t", a=2, t=half)
                    key, query = (x.rearrange("p (g a t) -> p g a t", a=2, t=half) for x in (f_key, hq_t))
                    v.tensor_tensor(d[:, :, 0], d[:, :, 0], key[:, :, 0], ALU.mult)
                    last = v.tensor_tensor(d[:, :, 1], d[:, :, 1], query[:, :, 1], ALU.mult)
                last.then_inc(s_x3, 1)
                for m in range(4):
                    dve.wait_ge(s_lv, i * 4 + (m + 1))
                    dve.wait_ge(s_sc, i * 4 + (m + 1))
                    bank = LEVEL_BANKS[m]
                    v.tensor_tensor(masked.rearrange("p l t -> p (l t)"), ps[:, bank:bank + 2, :].rearrange("p a n -> p (a n)"),
                                    level_mask, ALU.mult).then_inc(s_lvr, 1)
                    dve.wait_ge(s_lvr, i * 4 + (m + 1))
                    v.tensor_reduce(score_t[:, m], masked.rearrange("p l t -> p t l"), AX_X, ALU.add).then_inc(s_sc, 1)
                for r in range(2):
                    ada_tile(r, sums, i * 4 + (r + 2), i * 2 + (KT // 2 + 1))
                dve.wait_ge(s_eg, i + 1)
                me.link(v.tensor_scalar(g_exp, g_exp, 1.0, None, ALU.add))
                me.link(v.reciprocal(g_exp, g_exp))
                for h in range(2):
                    w = slice(h * 256, (h + 1) * 256)
                    last = v.scalar_tensor_tensor(out=g_t[:, w], in0=ps[:, 7, w], scalar=norm_col[:, ds(i * 2 + h, 1)],
                                                  in1=g_exp[:, w], op0=ALU.mult, op1=ALU.mult)
                last.then_inc(s_g, 1)
                dve.wait_ge(s_rs, i + 1)
                for m in range(4):
                    last = v.tensor_scalar(o_norm[:, m], ps[:, 5, m * P:(m + 1) * P], rstd[:, m:m + 1], None, ALU.mult)
                last.then_inc(s_on, 1)
                dve.wait_ge(s_tr, i + 1)
                dve.wait_ge(s_g, i + 2)
                v.tensor_tensor(hgrn_t[:, ds(i * 2, 2), :], ps[:, 6, :].rearrange("p (h t) -> p h t", h=2),
                                g_t.rearrange("p (h t) -> p h t", h=2), ALU.mult).then_inc(s_bt, 1)

            with me.loop(GATES, 4) as i:
                dve.wait_ge(s_ea, i + 2)
                me.link(v.tensor_scalar(ga_exp, ga_exp, 1.0, None, ALU.add))
                me.link(v.reciprocal(ga_exp, ga_exp))
                dve.wait_ge(s_eb, i + 2)
                me.link(v.tensor_scalar(gb_exp, gb_exp, 1.0, None, ALU.add))
                me.link(v.reciprocal(gb_exp, gb_exp))
                dve.wait_ge(s_a, i + 1)
                dve.wait_ge(s_mg, 1 + i)
                v.tensor_tensor(m_a, ps[:, 2, :], ga_exp, ALU.mult).then_inc(s_am, 1)
                dve.wait_ge(used[2], i + (1 + F_GATE[2] + 1))
                v.tensor_tensor(m_b, ps[:, 3, :], gb_exp, ALU.mult).then_inc(s_bm, 1)
                dve.wait_ge(s_am, i + 2)
                dve.wait_ge(s_bm, i + 2)
                v.tensor_tensor(merged_t[:, ds(i * 2, 2), :], m_a.rearrange("p (h t) -> p h t", h=2),
                                m_b.rearrange("p (h t) -> p h t", h=2), ALU.add).then_inc(s_mg, 1)

            dve.wait_ge(s_row, 1 + 16)
            dve.wait_ge(s_ln[0], 16)
            spare = pq_t[1]
            for n in range(4):
                c = slice(n * 512, (n + 1) * 512)
                me.link(v.scalar_tensor_tensor(out=spare, in0=scale2[:, c], scalar=1.0, in1=ln_slot[0][:, 1, c], op0=ALU.add, op1=ALU.mult))
                me.link(v.tensor_tensor(shift2[:, c], shift2[:, c], spare, ALU.add))
            me.link(v.scalar_tensor_tensor(out=scale2, in0=scale2, scalar=1.0, in1=ln_slot[0][:, 0], op0=ALU.add, op1=ALU.mult))
            gain2, bias2 = scale2, shift2

            dve.wait_ge(s_xr, 16)
            y = out_term
            with me.loop(2, 4) as i:
                for s in range(4):
                    dve.wait_ge(used[s], i + (1 + F_OUT[s] + 1))
                    dve.wait_ge(s_y, i * 4 + (1 + s))
                    c = ds((i * 4 + s) * COLS, COLS)
                    g = mod_rows[:, ds((i * 4 + s) * COLS, COLS)]
                    for b in range(BLOCKS):
                        last = v.scalar_tensor_tensor(out=y[:, b], in0=g, scalar=1.0, in1=ps[:, s, b * COLS:(b + 1) * COLS],
                                                      op0=ALU.add, op1=ALU.mult)
                    me.link(last)
                    v.scalar_tensor_tensor(out=xr[:, :, c], in0=xr[:, :, c], scalar=ALPHA, in1=y, op0=ALU.mult, op1=ALU.add)\
                        .then_inc(s_y, 1)
            dve.wait_ge(s_y, 1 + GATES)

            def ln_statistics(rows, b):
                for q in range(4):
                    me.step(v.bn_stats(ln_stats[:, q], rows[:, q * 512:(q + 1) * 512]))
                me.settle()
                me.link(v.bn_aggr(ln_mv[b], ln_stats.rearrange("p a c -> p (a c)")))
                v.tensor_scalar(ln_mv[b][:, 1:2], ln_mv[b][:, 1:2], LN_EPS, None, ALU.add).then_inc(s_var, 1)

            for b in range(BLOCKS):
                ln_statistics(xr[:, b], b)
            for b in range(BLOCKS):
                dve.wait_ge(s_xn, b + 1)
                me.link(v.tensor_tensor(h2[:, b], xr[:, b], gain2, ALU.mult))
                v.tensor_tensor(h2[:, b], h2[:, b], bias2, ALU.add).then_inc(s_h2, 1)
            for b in range(BLOCKS):
                me.link(v.tensor_tensor(xr[:, b], xr[:, b], ln_slot[0][:, 0], ALU.mult))
                me.link(v.tensor_tensor(xr[:, b], xr[:, b], ln_slot[0][:, 1], ALU.add))

            def spread(a, n):
                return a.unsqueeze(2).to_broadcast([P, n, TOPK])

            def top16(values, indices, source, reduced, first_wait):
                n = range(len(source))
                wait_alone(dve, *first_wait)
                for j in n:
                    me.step(v.max(values[j][:, 0:8], source[j]))
                wait_alone(dve, *me.reached())
                for j in n:
                    me.step(v.max_index(indices[j][:, 0:8], values[j][:, 0:8], source[j]))
                    me.step(v.match_replace(reduced[j], values[j][:, 0:8], source[j], LOWEST))
                wait_alone(dve, *me.reached())
                for j in n:
                    me.step(v.max(values[j][:, 8:16], reduced[j]))
                wait_alone(dve, *me.reached())
                for j in n:
                    last = v.max_index(indices[j][:, 8:16], values[j][:, 8:16], reduced[j])
                    if j < n[-1]:
                        me.step(last)
                return last

            def choose_experts(b, h, n, source, source_ready, signal):
                top16([top_v[:, c] for c in range(2)], [top_i[:, c] for c in range(2)], source,
                      [rest[:, c] for c in range(2)], source_ready).then_inc(signal[0], 1)
                dve.wait_ge(*signal)
                me.step(v.tensor_copy(top_if, top_i[:]))
                me.step(v.tensor_tensor(cand, spread(top_v[:, 0], TOPK), top_v[:, 1].unsqueeze(1).to_broadcast([P, TOPK, TOPK]), ALU.add))
                me.link(top16([best], [pos[:]], [cand.rearrange("p a c -> p (a c)")], [onehot[:, 0:256]], me.reached()))
                v.tensor_scalar(soft, best, best[:, 0:1], None, ALU.subtract).then_inc(s_sd, 1)
                me.step(v.tensor_scalar(hilo[:, 0], pos[:], 4, None, ALU.logical_shift_right))
                me.link(v.tensor_scalar(hilo[:, 1], pos[:], 15, None, ALU.bitwise_and))
                me.link(v.tensor_copy(hilo_f, hilo[:].rearrange("p c k -> p (c k)")))
                me.link(v.tensor_tensor(onehot.rearrange("p (k a) -> p k a", a=TOPK), spread(hilo_f, 2 * TOPK),
                                        iota.unsqueeze(1).to_broadcast([P, 2 * TOPK, TOPK]), ALU.is_equal))
                for c in range(2):
                    half = onehot[:, c * 256:(c + 1) * 256].rearrange("p (k a) -> p k a", a=TOPK)
                    me.step(v.tensor_tensor(half, half, top_if[:, c].unsqueeze(1).to_broadcast([P, TOPK, TOPK]), ALU.mult))
                me.settle()
                me.link(v.tensor_reduce(expert_f, onehot.rearrange("p (k a) -> p k a", a=TOPK), AX_X, ALU.add))
                me.link(v.scalar_tensor_tensor(out=expert_f[:, 0:TOPK], in0=expert_f[:, 0:TOPK], scalar=float(N_KEYS),
                                               in1=expert_f[:, TOPK:], op0=ALU.mult, op1=ALU.add))
                v.tensor_copy(expert[:, b, ds(h * TOPK, TOPK)], expert_f[:, 0:TOPK]).then_inc(s_ex, 1)
                dve.wait_ge(s_se, n + 1)
                me.link(v.tensor_reduce(soft_sum, soft, AX_X, ALU.add))
                me.link(v.reciprocal(soft_sum, soft_sum))
                v.tensor_scalar(gates[:, b, ds(h * TOPK, TOPK)], soft, soft_sum, None, ALU.mult).then_inc(s_gt, 1)

            def choose_late(h):
                me.link(v.tensor_copy(late, late_scores[:, ds(h * 2, 2), :]))
                choose_experts(1, h, h + HEADS, [late[:, c] for c in range(2)], me.reached(), (s_read, h + 1))

            def reduce_rows(b, heads, which):
                for e in which:
                    s = e % U_RING
                    dve.wait_ge(u_loaded[s], heads * (16 * TOPK // U_RING) + (e // U_RING + 1) * 16)
                    v.tensor_tensor_reduce(out=u_slot[s], in0=u_slot[s], in1=h2[:, b], scale=1.0, scalar=0.0,
                                           op0=ALU.mult, op1=ALU.add, accum_out=act[:, e:e + 1]).then_inc(u_used[s], 1)

            def weigh(b, h, heads):
                dve.wait_ge(s_gel, heads + 1)
                v.tensor_tensor(wgt, gel, gates[:, b, ds(h * TOPK, TOPK)], ALU.mult).then_inc(s_wgt, 1)

            def finish_rows(b, n):
                for s in range(V_RING):
                    dve.wait_ge(v_used[s], 1 + (b + 1) * SLOTS // V_RING)
                rows = h2[:, b]
                me.link(v.scalar_tensor_tensor(out=rows, in0=gate2, scalar=1.0, in1=ps[:, 4 * b:4 * b + 4, :].rearrange("p a n -> p (a n)"),
                                               op0=ALU.add, op1=ALU.mult))
                me.link(v.scalar_tensor_tensor(out=rows, in0=xr[:, b], scalar=ALPHA, in1=rows, op0=ALU.mult, op1=ALU.add))
                ln_statistics(rows, b)
                dve.wait_ge(s_std, n)
                me.link(v.tensor_scalar(rows, rows, ln_mv[b][:, 0:1], ln_rstd[b], ALU.subtract, ALU.mult))
                dve.wait_ge(s_ln[1], 16)
                me.link(v.tensor_tensor(rows, rows, ln_slot[1][:, 0], ALU.mult))
                v.tensor_tensor(rows, rows, ln_slot[1][:, 1], ALU.add).then_inc(s_fin, 1)

            for half in range(2):
                with me.loop(2, 2 * STEPS_OF_CHOICE) as i:
                    for s in range(2):
                        h = i * 2 + (half * 4 + s)
                        choose_experts(0, h, h, [ps[:, 2 + s, c * P:(c + 1) * P] for c in range(2)],
                                       (s_ks, i * 2 + (half * 4 + s + 1)), (s_top, i * 2 + (half * 4 + s + 2)))
                reduce_rows(0, 0, range(half * 8, half * 8 + 8))
            weigh(0, 0, 0)
            with me.loop(HEADS - 1, STEPS_OF_CHOICE + 1) as i:
                choose_late(i)
                reduce_rows(0, i + 1, range(TOPK))
                weigh(0, i + 1, i + 1)
            choose_late(HEADS - 1)
            reduce_rows(1, HEADS, range(TOPK))
            weigh(1, 0, HEADS)
            finish_rows(0, BLOCKS + 1)
            with me.loop(HEADS - 1, 0) as i:
                reduce_rows(1, i + (HEADS + 1), range(TOPK))
                weigh(1, i + 1, i + (HEADS + 1))
            finish_rows(1, BLOCKS + 2)


def kernel(x, c, w_ada, b_ada, w_in, hg_lb_logits, hg_norm_g, w_branch_a, w_branch_b, w_out,
           ln1_g, ln1_b, peer_wq, peer_subkeys, peer_u, peer_v, ln2_g, ln2_b):
    import concourse.bacc as bacc
    from concourse.bass_utils import run_bass_kernel_spmd

    def f32(a):
        return np.asarray(a)

    def chunked(w):
        rows, n = w.shape
        return w.reshape(rows // P, P, n // COLS, COLS).transpose(2, 1, 0, 3).reshape(n // COLS, P, rows // P * COLS)

    w = chunked(f32(w_in)[0])
    sb_q, sb_k, sb_v, hg_q, hg_f, hg_i, hg_g = (w[n * PAIRS:(n + 1) * PAIRS] for n in range(7))
    gate_a, gate_b = w[7 * PAIRS:7 * PAIRS + GATES], w[7 * PAIRS + GATES:]
    branches = np.concatenate([chunked(f32(w_branch_a)[0]), chunked(f32(w_branch_b)[0])], axis=2)

    def woven(*roles):
        return np.stack(roles, axis=1).reshape(-1, P, CHUNK)

    weights = np.concatenate([woven(sb_q, sb_k, sb_v), woven(hg_f, hg_q, hg_i, hg_g), woven(gate_a, gate_b, branches),
                              chunked(f32(w_out)[0]), chunked(f32(peer_wq)[0])])
    x = f32(x)[0]
    arrays = {
        "consts": constants(),
        "x_rows": x.reshape(BLOCKS, P, D_MODEL).transpose(1, 0, 2),
        "x_t": x.reshape(TOKENS, KT, P).transpose(2, 1, 0).reshape(P, CHUNK),
        "cond_cols": f32(c)[0].reshape(KT, P).T,
        "ada": f32(w_ada)[0],
        "ada_bias": f32(b_ada),
        "weights": weights.reshape(N_CHUNKS * P, CHUNK),
        "lb_logits": f32(hg_lb_logits).reshape(2, HEADS, HEAD_DIM).transpose(2, 0, 1),
        "norm_gain": f32(hg_norm_g)[0].reshape(HEADS, HEAD_DIM).T,
        "ln_rows": np.stack([f32(a)[0] for a in (ln1_g, ln1_b, ln2_g, ln2_b)]),
        "subkeys_t": f32(peer_subkeys)[0].reshape(2 * HEADS, N_KEYS, P).transpose(2, 0, 1),
        "expert_u": f32(peer_u)[0],
        "expert_v": f32(peer_v)[0],
    }
    nc = bacc.Bacc("TRN2", target_bir_lowering=False, num_devices=1)
    arrays = {n: np.ascontiguousarray(a) for n, a in arrays.items()}
    args = [nc.dram_tensor(n, a.shape, F32, kind="ExternalInput").ap() for n, a in arrays.items()]
    out = nc.dram_tensor("out", (TOKENS, D_MODEL), F32, kind="ExternalOutput").ap()
    block_kernel(nc, *args, out)
    r = run_bass_kernel_spmd(nc, [arrays], core_ids=[0])
    return r.results[0]["out"].reshape(1, TOKENS, D_MODEL)
```

```python
import math
from contextlib import ExitStack, contextmanager

import numpy as np

import concourse.bass as bass
from concourse import mybir

F32 = mybir.dt.float32
U32 = mybir.dt.uint32
ALU = mybir.AluOpType
ACT = mybir.ActivationFunctionType
AX_X = mybir.AxisListType.X
ds = bass.ds

P = 128
TOKENS = 256
BLOCKS = TOKENS // P
D_MODEL = 2048
KT = D_MODEL // P
HEADS = 8
HEAD_DIM = 128
COLS = 256
PAIRS = HEADS * HEAD_DIM // COLS
CHUNK = KT * COLS
BRANCH_KT = HEADS * HEAD_DIM // P
LEVELS = 7
ADA_COLS = 4096
TOPK = 16
SLOTS = HEADS * TOPK
N_KEYS = 128
U_RING, V_RING = 4, 8
VECTOR_ROWS = (9, 11, 13)
ALPHA = 2.0 ** 0.25
LN_EPS = 1e-5
RMS_EPS = 1e-6
Z_SCALE = 1.0 / math.sqrt(HEAD_DIM)
LOWEST = -3.0e38

ATTN0 = 0
HGRN0 = ATTN0 + 3 * PAIRS
GATE0 = HGRN0 + 4 * PAIRS
GATES = D_MODEL // COLS
OUT0 = GATE0 + 3 * GATES
QUERY0 = OUT0 + D_MODEL // COLS
N_CHUNKS = QUERY0 + D_MODEL // COLS

C_IDENT = 0
C_ONES = C_IDENT + P
C_LATER = C_ONES + P
C_BEFORE = C_LATER + P
C_LEVELS = C_BEFORE + 3 * P
C_IOTA = C_LEVELS + 8 * P
C_END = C_IOTA + TOPK


def constants():
    c = np.zeros((P, C_END), np.float32)
    s, t = np.arange(P)[:, None], np.arange(P)[None, :]
    c[:, C_IDENT:C_ONES] = s == t
    c[:, C_ONES:C_LATER] = 1.0
    c[:, C_LATER:C_BEFORE] = s > t
    before = c[:, C_BEFORE:C_LEVELS].reshape(P, 3, P)
    before[:, 0] = s < t
    before[:, 1] = 1.0
    before[:, 2] = s < t
    levels = c[:, C_LEVELS:C_IOTA].reshape(P, 8, P)
    levels[:, 0] = s == t
    for n in range(LEVELS):
        half = 1 << n
        levels[:, n + 1] = (s // (2 * half) == t // (2 * half)) & (s // half % 2 == 0) & (t // half % 2 == 1)
    c[:, C_IOTA:] = np.arange(TOPK)
    return c


class Steps:

    def __init__(self, engine, sem):
        self.engine, self.sem, self.base, self.n = engine, sem, 0, 0

    def step(self, instruction):
        instruction.then_inc(self.sem, 1)
        self.n += 1

    def settle(self):
        self.engine.wait_ge(*self.reached())

    def reached(self):
        return self.sem, self.base + self.n

    def link(self, instruction):
        self.step(instruction)
        self.settle()

    @contextmanager
    def loop(self, count, steps):
        before = self.base + self.n
        with self.engine.Fori(0, count) as i:
            self.base, self.n = i * steps + before, 0
            yield i
            assert self.n == steps, (self.n, steps)
        self.base, self.n = before + count * steps, 0


def block_kernel(nc, consts, x_rows, x_t, cond_cols, ada, ada_bias, weights, lb_logits, norm_gain,
                 ln_rows, subkeys_t, expert_u, expert_v, out):
    with ExitStack() as ctx:
        def sb(name, shape, dt=F32):
            return ctx.enter_context(nc.sbuf_tensor(name, shape, dt))

        def sem(name):
            return ctx.enter_context(nc.semaphore(name))

        from_one = []

        def sem1(name):
            from_one.append(sem(name))
            return from_one[-1]

        arena = sb("arena", [P, 7 * CHUNK])
        ring = [arena[:, s * CHUNK:(s + 1) * CHUNK].rearrange("p (k n) -> p k n", k=KT) for s in range(4)]
        ada_slot = [arena[:, (4 + s) * CHUNK:(5 + s) * CHUNK] for s in range(2)]
        branch_in = arena[:, 6 * CHUNK:7 * CHUNK].rearrange("p (a k t) -> p a k t", a=2, k=BRANCH_KT)
        attn_t, hgrn_t = branch_in[:, 0], branch_in[:, 1]
        h2_t = arena[:, 6 * CHUNK:7 * CHUNK].rearrange("p (k t) -> p k t", k=KT)
        ln_slot = [arena[:, c * CHUNK:(c + 1) * CHUNK].rearrange("p (a n) -> p a n", a=2) for c in (4, 6)]

        buf_a = sb("buf_a", [P, CHUNK])
        h_t = buf_a[:].rearrange("p (k t) -> p k t", k=KT)
        xr = buf_a[:].rearrange("p (b n) -> p b n", b=BLOCKS)
        buf_b = sb("buf_b", [P, CHUNK])
        merged_t = buf_b[:].rearrange("p (k t) -> p k t", k=KT)
        decay = buf_b[:].rearrange("p (l m t) -> p l m t", l=8, m=4)
        h2 = buf_b[:].rearrange("p (b n) -> p b n", b=BLOCKS)
        mod_rows = sb("mod_rows", [P, 4 * D_MODEL])
        gate1, shift2, scale2, gate2 = (mod_rows[:, n * D_MODEL:(n + 1) * D_MODEL] for n in range(4))

        row = D_MODEL
        u_slot = [arena[:, s * row:(s + 1) * row] for s in (4, 5, 6, 7)]
        v_slot = [arena[:, s * row:(s + 1) * row] for s in (8, 9, 10, 11)] + [shift2, scale2]\
            + [arena[:, s * row:(s + 1) * row] for s in (0, 1)]
        late_scores = gate1.rearrange("p (c n) -> p c n", c=2 * HEADS)

        cst = sb("cst", [P, C_END])
        ident, ones = cst[:, C_IDENT:C_ONES], cst[:, C_ONES:C_LATER]
        later = cst[:, C_LATER:C_BEFORE]
        before = cst[:, C_BEFORE:C_LEVELS]
        level_mask = cst[:, C_LEVELS:C_IOTA]
        iota = cst[:, C_IDENT + C_IOTA:C_END]

        cols = sb("cols", [P, 128])
        cond_in, cond_sig, cond = cols[:, 0:16], cols[:, 16:32], cols[:, 32:48]
        shift1, scale1 = cols[:, 48:64], cols[:, 64:80]
        lb, lb_rest, norm_col = cols[:, 80:88], cols[:, 88:96], cols[:, 96:104]
        rms_eps = cols[:, 120:121]
        first_act = cols[:, 124:124 + U_RING]
        logits = cols[:, 104:120].rearrange("p (a h) -> p a h", a=2)
        small = sb("small", [P, 88])
        lb_max, lb_sum = small[:, 0:8], small[:, 8:16]
        sq_sum, rstd = small[:, 16:20], small[:, 20:24]
        ln_stats = [a.rearrange("p (a c) -> p a c", a=4) for a in (small[:, 24:48], small[:, 64:88])]
        ln_mv = [small[:, 48 + 2 * b:50 + 2 * b] for b in range(BLOCKS)]
        ln_rstd = [small[:, 52 + b:53 + b] for b in range(BLOCKS)]
        ln_log = [small[:, 54 + b:55 + b] for b in range(BLOCKS)]

        WORK = 5332
        work = sb("work", [P, WORK])
        at = [0]

        def part(n):
            at[0] += n
            assert at[0] <= WORK, at[0]
            return work[:, at[0] - n:at[0]]

        q_t = part(512).rearrange("p (h t) -> p h t", h=2)
        k_t = part(512).rearrange("p (h t) -> p h t", h=2)
        v_rows = part(512).rearrange("p (b n) -> p b n", b=BLOCKS)
        a_exp = part(768).rearrange("p (h s) -> p h s", h=2)
        a_pen = part(768).rearrange("p (h s) -> p h s", h=2)
        a_log = part(768).rearrange("p (h s) -> p h s", h=2)
        a_w = part(768).rearrange("p (h s) -> p h s", h=2)
        at[0] = 0
        f_gate, f_key, f_log, f_cum, hq_t = (part(512) for _ in range(5))
        hv_rows = part(512).rearrange("p (b n) -> p b n", b=BLOCKS)
        score_t = part(512).rearrange("p (m t) -> p m t", m=4)
        cross_t = part(256).rearrange("p (h t) -> p h t", h=2)
        masked = part(1024).rearrange("p (l t) -> p l t", l=8)
        g_exp, g_t, o_norm = f_log, f_gate, f_cum.rearrange("p (m t) -> p m t", m=4)
        at[0] = 0
        ga_exp, gb_exp, m_a, m_b = (part(512) for _ in range(4))
        at[0] = 0
        sk = part(2048).rearrange("p (c n) -> p c n", c=2 * HEADS)
        pq_t = [part(512) for _ in range(2)]
        out_term = pq_t[0].rearrange("p (b n) -> p b n", b=BLOCKS)
        rest = part(256).rearrange("p (c n) -> p c n", c=2)
        cand = part(256).rearrange("p (a c) -> p a c", a=TOPK)
        onehot = part(512)
        top_v = part(32).rearrange("p (c k) -> p c k", c=2)
        top_if = part(32).rearrange("p (c k) -> p c k", c=2)
        best, soft = part(TOPK), part(TOPK)
        hilo_f, expert_f = part(32), part(32)
        soft_sum = part(1)
        top_i = sb("top_i", [P, 2, TOPK], U32)
        pos = sb("pos", [P, TOPK], U32)
        hilo = sb("hilo", [P, 2, TOPK], U32)
        expert = sb("expert", [P, BLOCKS, SLOTS], U32)
        gates = sb("gates", [P, BLOCKS, SLOTS])
        late = pq_t[0][:, 0:256].rearrange("p (c n) -> p c n", c=2)
        act, gel, wgt = part(TOPK), part(TOPK), part(TOPK)
        diag = part(V_RING * P).rearrange("p (s n) -> p s n", s=V_RING)
        u_now, v_now = sb("u_now", [P, TOPK], U32), sb("v_now", [P, TOPK], U32)

        ps = ctx.enter_context(nc.psum_tensor("ps", [P, 8, 512], F32))

        s_const, s_x, s_cols = sem("const_loaded"), sem("x_loaded"), sem("cols_loaded")
        s_bias = [sem("bias1_loaded"), sem("bias2_loaded")]
        loaded = [sem(f"slot{s}_loaded") for s in range(4)]
        used = [sem1(f"slot{s}_used") for s in range(4)]
        ada_loaded = [sem(f"ada{s}_loaded") for s in range(2)]
        ada_used = [sem1(f"ada{s}_used") for s in range(2)]
        dve_step, act_step = sem("vector_steps"), sem("scalar_steps")
        s_cleared, s_zero, s_sig, s_cond = sem("sums_cleared"), sem("mod_rows_cleared"), sem("cond_exp"), sem("cond_ready")
        s_mod, s_modc, s_h = sem("mod_products"), sem("mod_cols_ready"), sem("h_ready")
        s_q, s_k, s_v, s_z, s_log = sem1("q_ready"), sem1("k_ready"), sem1("v_ready"), sem("scores"), sem("log_ready")
        s_pen, s_tail, s_u, s_wexp, s_w = sem("penalty"), sem("tails"), sem("w_log"), sem("w_exp"), sem("w_ready")
        s_pv, s_at = sem("attn_products"), sem1("attn_ready")
        s_ef, s_f, s_lf, s_d, s_x2 = sem("f_exp"), sem("f_ready"), sem("f_log_ready"), sem("decay_logs"), sem("decay_exp")
        s_hq, s_hv, s_eg, s_g, s_x3 = sem("hq_ready"), sem("hv_ready"), sem("g_exp"), sem1("g_ready"), sem("factors")
        s_lv, s_lvr, s_sc = sem("level_products"), sem("levels_read"), sem1("hgrn_scores")
        s_cr, s_crr, s_o, s_rs = sem("cross_products"), sem("cross_ready"), sem("o_products"), sem("rstd_ready")
        s_on, s_tr, s_bt = sem("o_normed"), sem("o_transposed"), sem1("hgrn_ready")
        s_ea, s_eb, s_a, s_am, s_bm = sem1("ga_exp"), sem1("gb_exp"), sem("branch_a"), sem1("a_merged"), sem1("b_merged")
        s_mm, s_row, s_mg = sem("mod_row_products"), sem1("mod_rows_ready"), sem1("merged_ready")
        s_xr, s_ln, s_sk = sem("x_rows_loaded"), [sem("ln1_loaded"), sem("ln2_loaded")], sem("subkeys_loaded")
        s_half, s_cen = sem("first_half_summed"), sem("rows_read")
        s_y, s_var, s_std, s_xn, s_fin = sem1("out_added"), sem("ln_var"), sem("ln_rstd"), sem("x_normed"), sem("rows_final")
        s_h2, s_h2p, s_h2t = sem("h2_ready"), sem("h2_transposed"), sem("h2t_ready")
        s_pq, s_ks, s_top, s_late = sem("pq_ready"), sem("key_scores"), sem1("scores_read"), sem1("late_scores_kept")
        s_sd, s_se, s_ex, s_gt = sem("soft_in"), sem("soft_exp"), sem("experts_ready"), sem("gates_ready")
        s_read, s_first = sem("late_scores_read"), sem("first_sums")
        s_now = sem("indices_set")
        u_loaded = [sem(f"u{s}_loaded") for s in range(U_RING)]
        u_used = [sem1(f"u{s}_used") for s in range(U_RING)]
        v_loaded = [sem(f"v{s}_loaded") for s in range(V_RING)]
        v_used = [sem1(f"v{s}_used") for s in range(V_RING)]
        s_gel, s_wgt, s_dg, s_out = sem("gelu_ready"), sem("weights_ready"), sem("diag_ready"), sem("out_stored")

        block = ctx.enter_context(nc.Block())

        halves = [slice(0, D_MODEL // 2), slice(D_MODEL // 2, D_MODEL)]

        def wait_alone(engine, sem, value):
            engine.wait_ge(sem, value)
            engine.nop(nofuse=True)

        F_ATTN = (4, 4, 4, 4)
        F_HGRN = tuple(n + m * PAIRS for n, m in zip(F_ATTN, (1, 1, 1, 0)))
        F_GATE = tuple(n + PAIRS for n in F_HGRN)
        F_OUT = tuple(n + m * GATES for n, m in zip(F_GATE, (1, 1, 1, 0)))
        F_QUERY = tuple(n + 2 for n in F_OUT)
        F_END = tuple(n + m * 4 for n, m in zip(F_QUERY, (1, 1, 0, 0)))

        @block.sync
        def _(sp):
            sp.dma_start(cols[:, 0:16], cond_cols).then_inc(s_cols, 16)
            sp.dma_start(logits, lb_logits).then_inc(s_cols, 16)
            sp.dma_start(norm_col, norm_gain).then_inc(s_cols, 16)
            with sp.Fori(0, 4) as i:
                for s in range(4):
                    sp.wait_ge(used[s], 1 + i)
                    sp.dma_start(arena[:, s * CHUNK:(s + 1) * CHUNK], ada[ds((i * 4 + s) * P, P), 0:ADA_COLS])\
                        .then_inc(loaded[s], 16)
            sp.dma_start(cst[:], consts).then_inc(s_const, 16)
            sp.dma_start(buf_a[:], x_t).then_inc(s_x, 16)

            def stream(turns, first, slots, filled):
                with sp.Fori(0, turns) as i:
                    for s in slots:
                        sp.wait_ge(used[s], i + (1 + filled[s]))
                        sp.dma_start(arena[:, s * CHUNK:(s + 1) * CHUNK],
                                     weights[ds((i * len(slots) + first + s) * P, P), :]).then_inc(loaded[s], 16)

            stream(PAIRS, ATTN0, range(3), F_ATTN)
            stream(PAIRS, HGRN0, range(4), F_HGRN)
            stream(GATES, GATE0, range(3), F_GATE)
            sp.wait_ge(used[1], 1 + F_OUT[1])
            sp.dma_start(xr, x_rows).then_inc(s_xr, 16)
            stream(2, OUT0, range(4), F_OUT)
            sp.wait_ge(s_mg, 1 + GATES)
            sp.dma_start(sk, subkeys_t).then_inc(s_sk, 16)
            stream(4, QUERY0, range(2), F_QUERY)
            for s in range(2):
                sp.wait_ge(used[s], 1 + F_END[s])
            sp.dma_start(ln_slot[1], ln_rows[2:4, :].partition_broadcast(P)).then_inc(s_ln[1], 16)
            for b in range(BLOCKS):
                for j, c in enumerate(halves):
                    sp.wait_ge(s_fin, 2 * b + j + 1)
                    sp.dma_start(out[b * P:(b + 1) * P, c], h2[:, b, c]).then_inc(s_out, 16)
            sp.wait_ge(s_out, 16 * 2 * BLOCKS)

        @block.gpsimd
        def _(pool):
            for x in from_one:
                pool.sem_inc(x, 1)
            nc.gpsimd.memset(mod_rows[:], 0.0).then_inc(s_zero, 1)
            pool.wait_ge(s_zero, 1)
            pool.dma_start(mod_rows[0:1, :], ada_bias[0:1, ADA_COLS:]).then_inc(s_bias[1], 16)
            pool.wait_ge(used[3], 1 + 2)
            for g in range(2):
                with pool.Fori(0, KT // 2) as i:
                    for s in range(2):
                        pool.wait_ge(ada_used[s], i + (1 + g * KT // 2))
                        pool.dma_start(ada_slot[s], ada[ds((i * 2 + s) * P, P), (g + 1) * ADA_COLS:(g + 2) * ADA_COLS])\
                            .then_inc(ada_loaded[s], 16)
            for s in range(2):
                pool.wait_ge(ada_used[s], 1 + KT)
            pool.dma_start(ln_slot[0], ln_rows[0:2, :].partition_broadcast(P)).then_inc(s_ln[0], 16)

            def take(indices, ring_loaded, b, h, heads, n):
                if ring_loaded:
                    per_head = 16 * TOPK // len(ring_loaded)
                    for x in ring_loaded:
                        wait_alone(pool, x, heads * per_head)
                pool.tensor_copy(indices[:], expert[:, b, ds(h * TOPK, TOPK)]).then_inc(s_now, 1)
                wait_alone(pool, s_now, heads * 2 + n)

            def gather_rows(table, indices, slots, ring_loaded, ring_used, heads, which):
                for e in which:
                    s = e % len(ring_used)
                    wait_alone(pool, ring_used[s], heads * (TOPK // len(ring_used)) + (1 + e // len(ring_used)))
                    pool.indirect_dma_start(slots[s], None, table,
                                            bass.IndirectOffsetOnAxis(ap=indices[:, e:e + 1], axis=0)).then_inc(ring_loaded[s], 16)

            def gather_u(heads, which=range(TOPK)):
                gather_rows(expert_u, u_now, u_slot, u_loaded, u_used, heads, which)

            def gather_v(heads, which=range(TOPK)):
                gather_rows(expert_v, v_now, v_slot, v_loaded, v_used, heads, which)

            def gather(b, h, heads):
                take(u_now, u_loaded, b, h, heads, 1)
                gather_u(heads)
                take(v_now, v_loaded, b, h, heads, 2)
                gather_v(heads)

            pool.wait_ge(s_ex, 1)
            take(u_now, [], 0, 0, 0, 1)
            take(v_now, [], 0, 0, 0, 2)
            gather_u(0, range(U_RING))
            for n in range(1, TOPK // U_RING):
                gather_u(0, range(n * U_RING, (n + 1) * U_RING))
                gather_v(0, range(2 * n - 2, 2 * n))
            pool.wait_ge(used[0], 1 + F_END[0])
            gather_v(0, range(V_RING - 2, V_RING))
            pool.wait_ge(s_ex, 2)
            take(u_now, u_loaded, 0, 1, 1, 1)
            gather_u(1, range(U_RING))
            gather_v(0, range(V_RING, V_RING + 4))
            for n in range(4):
                gather_u(1, [U_RING + n])
                gather_v(0, [V_RING + 4 + n])
            gather_u(1, range(2 * U_RING, TOPK))
            take(v_now, v_loaded, 0, 1, 1, 2)
            gather_v(1)
            with pool.Fori(0, HEADS - 2) as i:
                pool.wait_ge(s_ex, i + 3)
                gather(0, i + 2, i + 2)
            pool.wait_ge(s_ex, BLOCKS * HEADS)
            with pool.Fori(0, HEADS) as i:
                gather(1, i, i + HEADS)

        @block.scalar
        def _(act_e):
            me = Steps(act_e, act_step)
            run = nc.scalar.activation
            act_e.wait_ge(s_cleared, 1)
            act_e.dma_start(buf_b[0:1, :], ada_bias[0:1, 0:ADA_COLS]).then_inc(s_bias[0], 16)
            act_e.wait_ge(s_cols, 48)
            run(cond_sig, cond_in, ACT.Exp, scale=-1.0).then_inc(s_sig, 1)
            act_e.wait_ge(s_cond, 1)
            run(logits, logits, ACT.Exp).then_inc(s_sig, 1)
            act_e.wait_ge(s_modc, 1)
            act_e.wait_ge(s_x, 16)
            for k in range(KT // 2, KT):
                run(h_t[:, k], h_t[:, k], ACT.Identity, bias=shift1[:, k:k + 1], scale=scale1[:, k:k + 1]).then_inc(s_h, 1)

            with me.loop(PAIRS, 2) as i:
                act_e.wait_ge(used[0], i + (1 + F_ATTN[0] + 1))
                run(q_t, ps[:, 0, :].rearrange("p (h t) -> p h t", h=2), ACT.Copy, scale=Z_SCALE).then_inc(s_q, 1)
                act_e.wait_ge(s_z, i + 1)
                me.link(run(a_exp, ps[:, 3:5, 0:384], ACT.Abs))
                me.link(run(a_exp, a_exp, ACT.Exp, scale=-1.0))
                run(a_log, a_exp, ACT.Ln, bias=1.0).then_inc(s_log, 1)
                act_e.wait_ge(s_u, i + 1)
                run(a_w, a_w, ACT.Exp).then_inc(s_wexp, 1)
                act_e.wait_ge(used[2], i + (1 + F_ATTN[2] + 1))
                run(v_rows, ps[:, 2, :].rearrange("p (b n) -> p b n", b=2), ACT.Copy).then_inc(s_v, 1)
                act_e.wait_ge(s_pv, i + 1)
                run(attn_t[:, ds(i * 2, 2), :], ps[:, 7, :].rearrange("p (h t) -> p h t", h=2), ACT.Copy).then_inc(s_at, 1)

            with me.loop(PAIRS, 5) as i:
                act_e.wait_ge(used[0], i + (1 + F_HGRN[0] + 1))
                act_e.wait_ge(s_bt, 1 + i)
                run(f_gate, ps[:, 0, :], ACT.Exp, scale=-1.0).then_inc(s_ef, 1)
                act_e.wait_ge(s_f, i * 2 + 2)
                run(f_log, f_gate, ACT.Ln).then_inc(s_lf, 1)
                act_e.wait_ge(used[1], i + (1 + F_HGRN[1] + 1))
                run(hq_t, ps[:, 1, :], ACT.Copy).then_inc(s_hq, 1)
                act_e.wait_ge(s_d, i + 1)
                run(decay[:, 0:4], decay[:, 0:4], ACT.Exp).then_inc(s_x2, 1)
                run(decay[:, 4:8], decay[:, 4:8], ACT.Exp).then_inc(s_x2, 1)
                act_e.wait_ge(used[2], i + (1 + F_HGRN[2] + 1))
                run(hv_rows, ps[:, 2, :].rearrange("p (b n) -> p b n", b=2), ACT.Copy).then_inc(s_hv, 1)
                act_e.wait_ge(s_cr, i + 1)
                run(cross_t, ps[:, 2, 0:256].rearrange("p (h t) -> p h t", h=2), ACT.Copy).then_inc(s_crr, 1)
                act_e.wait_ge(s_o, i + 1)
                for m in range(4):
                    me.step(run(masked[:, m], ps[:, 5, m * P:(m + 1) * P], ACT.Square, accum_out=sq_sum[:, m:m + 1]))
                me.settle()
                act_e.wait_ge(s_cleared, 2)
                me.link(run(rstd, sq_sum, ACT.Ln, scale=1.0 / HEAD_DIM, bias=rms_eps))
                run(rstd, rstd, ACT.Exp, scale=-0.5).then_inc(s_rs, 1)
                act_e.wait_ge(used[3], i + (1 + F_HGRN[3] + 1))
                run(g_exp, ps[:, 7, :], ACT.Exp, scale=-1.0).then_inc(s_eg, 1)

            with me.loop(GATES, 0) as i:
                act_e.wait_ge(used[0], i + (1 + F_GATE[0] + 1))
                act_e.wait_ge(s_am, 1 + i)
                run(ga_exp, ps[:, 0, :], ACT.Exp, scale=-1.0).then_inc(s_ea, 1)
                act_e.wait_ge(used[1], i + (1 + F_GATE[1] + 1))
                act_e.wait_ge(s_bm, 1 + i)
                run(gb_exp, ps[:, 1, :], ACT.Exp, scale=-1.0).then_inc(s_eb, 1)
                for n in range(2):
                    act_e.wait_ge(s_mm, i * 2 + (n + 1))
                    run(mod_rows[:, ds((i * 2 + n) * 512, 512)], ps[:, 5 + n, :], ACT.Copy).then_inc(s_row, 1)

            def rstd_of_ln(b, n):
                act_e.wait_ge(s_var, n)
                me.link(run(ln_log[b], ln_mv[b][:, 1:2], ACT.Ln))
                run(ln_rstd[b], ln_log[b], ACT.Exp, scale=-0.5).then_inc(s_std, 1)

            for b in range(BLOCKS):
                rstd_of_ln(b, b + 1)
            for b in range(BLOCKS):
                for g in range(4):
                    act_e.wait_ge(s_h2p, b * 4 + g + 1)
                    run(h2_t[:, 4 * g:4 * g + 4, b * P:(b + 1) * P], ps[:, 4 + g, :].rearrange("p (k t) -> p k t", k=4), ACT.Copy)\
                        .then_inc(s_h2t, 1)

            for b in range(BLOCKS):
                act_e.wait_ge(s_std, b + 1)
                me.link(run(ln_log[b], ln_mv[b][:, 0:1], ACT.Copy, scale=-1.0))
                me.link(run(ln_log[b], ln_log[b], ACT.Copy, scale=ln_rstd[b]))
                act_e.wait_ge(s_cen, b + 1)
                run(xr[:, b], xr[:, b], ACT.Identity, bias=ln_log[b], scale=ln_rstd[b]).then_inc(s_xn, 1)
            with me.loop(2, 0) as i:
                for s in range(4):
                    act_e.wait_ge(used[s % 2], i * 2 + (1 + F_QUERY[s % 2] + s // 2 + 1))
                    run(pq_t[s % 2], ps[:, s % 2, :], ACT.Copy).then_inc(s_pq, 1)
                    act_e.wait_ge(s_ks, i * 4 + (s + 1))
                    run(late_scores[:, ds((i * 4 + s) * 2, 2), :], ps[:, 4 + s % 2, 0:256].rearrange("p (c n) -> p c n", c=2), ACT.Copy)\
                        .then_inc(s_late, 1)
                    act_e.wait_ge(s_sd, i * 4 + (s + 1))
                    run(soft, soft, ACT.Exp).then_inc(s_se, 1)

            def soft_exp(n):
                act_e.wait_ge(s_sd, n)
                run(soft, soft, ACT.Exp).then_inc(s_se, 1)

            def expert_weights(heads, first=False, skip=()):
                if first:
                    act_e.wait_ge(s_first, TOPK // U_RING)
                else:
                    act_e.wait_ge(u_used[U_RING - 1], heads * (TOPK // U_RING) + (1 + TOPK // U_RING))
                run(gel, act, ACT.Gelu).then_inc(s_gel, 1)
                act_e.wait_ge(s_wgt, heads + 1)
                for e in range(TOPK):
                    if e in skip:
                        continue
                    s = e % V_RING
                    act_e.wait_ge(v_used[s], heads * (TOPK // V_RING) + (1 + e // V_RING))
                    run(diag[:, s], ident, ACT.Copy, scale=wgt[:, e:e + 1]).then_inc(s_dg, 1)

            expert_weights(0, first=True)
            with me.loop(HEADS - 1, 0) as i:
                soft_exp(i + (HEADS + 1))
                expert_weights(i + 1)
            soft_exp(2 * HEADS)
            expert_weights(HEADS)
            rstd_of_ln(0, BLOCKS + 1)
            with me.loop(HEADS - 2, 0) as i:
                expert_weights(i + (HEADS + 1))
            expert_weights(2 * HEADS - 1, skip=VECTOR_ROWS)
            rstd_of_ln(1, BLOCKS + 2)

        STEPS_OF_CHOICE = 26
        LEVEL_BANKS = (3, 5, 0, 3)

        @block.tensor
        def _(pe):
            mm = nc.tensor.matmul

            def project_t(bank, slot, rhs, tiles=KT, first=0, halves=range(2)):
                for c in halves:
                    for k in range(tiles):
                        last = mm(ps[:, bank, c * TOKENS:(c + 1) * TOKENS], ring[slot][:, first + k, c * P:(c + 1) * P],
                                  rhs[:, k, :], start=(k == 0), stop=(k == tiles - 1))
                return last

            def project_rows(bank, slot, lhs, blocks=range(BLOCKS)):
                for b in blocks:
                    for k in range(KT):
                        last = mm(ps[:, bank, b * COLS:(b + 1) * COLS], lhs[:, k, b * P:(b + 1) * P],
                                  ring[slot][:, k, :], start=(k == 0), stop=(k == KT - 1))
                return last

            pe.wait_ge(s_const, 16)
            pe.wait_ge(used[3], 1 + F_ATTN[3])
            for k in range(2 * KT):
                last = mm(ps[:, 0, k:k + 1], buf_b[:, k * P:(k + 1) * P], ones[:, 0:1], start=True, stop=True)
            last.then_inc(s_mod, 1)
            pe.wait_ge(s_h, KT)

            with pe.Fori(0, PAIRS) as i:
                pe.wait_ge(loaded[0], i * 16 + (F_ATTN[0] + 1) * 16)
                pe.wait_ge(s_q, 1 + i)
                project_t(0, 0, h_t).then_inc(used[0], 1)
                pe.wait_ge(loaded[1], i * 16 + (F_ATTN[1] + 1) * 16)
                pe.wait_ge(s_k, 1 + i)
                project_t(1, 1, h_t).then_inc(used[1], 1)
                pe.wait_ge(s_q, i + 2)
                pe.wait_ge(s_k, i + 2)
                for h in range(2):
                    mm(ps[:, 3 + h, 0:256], k_t[:, h, 0:P], q_t[:, h, :], start=True, stop=True)
                    last = mm(ps[:, 3 + h, 256:384], k_t[:, h, P:2 * P], q_t[:, h, P:2 * P], start=True, stop=True)
                last.then_inc(s_z, 1)
                pe.wait_ge(loaded[2], i * 16 + (F_ATTN[2] + 1) * 16)
                pe.wait_ge(s_v, 1 + i)
                project_rows(2, 2, h_t, [0])
                pe.wait_ge(s_pen, i + 1)
                for h in range(2):
                    mm(ps[:, 5 + h, 0:384], later, a_pen[:, h, :], start=True, stop=False, skip_group_check=True)
                    last = mm(ps[:, 5 + h, P:2 * P], ones, a_pen[:, h, 256:384], start=False, stop=True, skip_group_check=True)
                last.then_inc(s_tail, 1)
                project_rows(2, 2, h_t, [1]).then_inc(used[2], 1)
                pe.wait_ge(s_v, i + 2)
                pe.wait_ge(s_w, i + 1)
                pe.wait_ge(s_at, 1 + i)
                for h in range(2):
                    mm(ps[:, 7, h * 256:(h + 1) * 256], v_rows[:, 0, h * P:(h + 1) * P], a_w[:, h, 0:256],
                       start=True, stop=False, skip_group_check=True)
                    last = mm(ps[:, 7, h * 256 + P:(h + 1) * 256], v_rows[:, 1, h * P:(h + 1) * P], a_w[:, h, 256:384],
                              start=False, stop=True, skip_group_check=True)
                last.then_inc(s_pv, 1)

            pe.wait_ge(s_at, 1 + PAIRS)
            with pe.Fori(0, PAIRS) as i:
                pe.wait_ge(loaded[0], i * 16 + (F_HGRN[0] + 1) * 16)
                project_t(0, 0, h_t).then_inc(used[0], 1)
                pe.wait_ge(loaded[1], i * 16 + (F_HGRN[1] + 1) * 16)
                project_t(1, 1, h_t).then_inc(used[1], 1)
                pe.wait_ge(loaded[2], i * 16 + (F_HGRN[2] + 1) * 16)
                project_rows(2, 2, h_t).then_inc(used[2], 1)
                pe.wait_ge(s_x3, i + 1)
                pe.wait_ge(s_hv, i + 1)
                for h in range(2):
                    last = mm(ps[:, 2, h * P:(h + 1) * P], decay[:, 0, 2 * h], decay[:, 0, 2 * h + 1], start=True, stop=True)
                last.then_inc(s_cr, 1)
                for m in range(4):
                    bank = LEVEL_BANKS[m]
                    if m == 3:
                        pe.wait_ge(s_lvr, i * 4 + 1)
                    mm(ps[:, bank, 0:P], f_key[:, m * P:(m + 1) * P], hq_t[:, m * P:(m + 1) * P], start=True, stop=True)
                    for n in range(1, 8):
                        last = mm(ps[:, bank + n // 4, n % 4 * P:(n % 4 + 1) * P], decay[:, n, m], decay[:, n, m],
                                  start=True, stop=True)
                    last.then_inc(s_lv, 1)
                pe.wait_ge(loaded[3], i * 16 + (F_HGRN[3] + 1) * 16)
                pe.wait_ge(s_g, 1 + i)
                project_t(7, 3, h_t, halves=[0])
                pe.wait_ge(s_crr, i + 1)
                pe.wait_ge(s_lvr, i * 4 + 2)
                for m in range(4):
                    h, b = m // 2, m % 2
                    pe.wait_ge(s_sc, i * 4 + (m + 2))
                    last = mm(ps[:, 5, m * P:(m + 1) * P], score_t[:, m], hv_rows[:, b, h * P:(h + 1) * P],
                              start=True, stop=(b == 0))
                    if b:
                        last = mm(ps[:, 5, m * P:(m + 1) * P], cross_t[:, h], hv_rows[:, 0, h * P:(h + 1) * P],
                                  start=False, stop=True)
                last.then_inc(s_o, 1)
                project_t(7, 3, h_t, halves=[1]).then_inc(used[3], 1)
                pe.wait_ge(s_on, i + 1)
                for m in range(4):
                    last = nc.tensor.transpose(ps[:, 6, m * P:(m + 1) * P], o_norm[:, m], ident)
                last.then_inc(s_tr, 1)

            pe.wait_ge(s_bt, 1 + PAIRS)
            for s in range(2):
                pe.wait_ge(ada_used[s], 1 + KT)
            with pe.Fori(0, GATES) as i:
                pe.wait_ge(loaded[0], i * 16 + (F_GATE[0] + 1) * 16)
                pe.wait_ge(s_ea, 1 + i)
                project_t(0, 0, h_t).then_inc(used[0], 1)
                pe.wait_ge(loaded[1], i * 16 + (F_GATE[1] + 1) * 16)
                pe.wait_ge(s_eb, 1 + i)
                project_t(1, 1, h_t).then_inc(used[1], 1)
                pe.wait_ge(loaded[2], i * 16 + (F_GATE[2] + 1) * 16)
                pe.wait_ge(s_am, 1 + i)
                project_t(2, 2, attn_t, BRANCH_KT).then_inc(s_a, 1)
                pe.wait_ge(s_bm, 1 + i)
                project_t(3, 2, hgrn_t, BRANCH_KT, BRANCH_KT).then_inc(used[2], 1)
                pe.wait_ge(s_row, i * 2 + 1)
                for n in range(2):
                    mm(ps[:, 5 + n, :], ones, mod_rows[:, ds((i * 2 + n) * 512, 512)], start=True, stop=True).then_inc(s_mm, 1)

            pe.wait_ge(s_mg, 1 + GATES)
            with pe.Fori(0, 2) as i:
                for s in range(4):
                    pe.wait_ge(loaded[s], i * 16 + (F_OUT[s] + 1) * 16)
                    pe.wait_ge(s_y, i * 4 + 1)
                    project_rows(s, s, merged_t).then_inc(used[s], 1)

            for b in range(BLOCKS):
                pe.wait_ge(s_h2, b + 1)
                for g in range(4):
                    if b:
                        pe.wait_ge(s_h2t, (b - 1) * 4 + g + 1)
                    for k in range(4):
                        last = nc.tensor.transpose(ps[:, 4 + g, k * P:(k + 1) * P], h2[:, b, (4 * g + k) * P:(4 * g + k + 1) * P], ident)
                    last.then_inc(s_h2p, 1)

            pe.wait_ge(s_h2t, 4 * BLOCKS)
            pe.wait_ge(s_sk, 16)
            with pe.Fori(0, 2) as i:
                for s in range(4):
                    pe.wait_ge(loaded[s % 2], i * 32 + (F_QUERY[s % 2] + s // 2 + 1) * 16)
                    project_t(s % 2, s % 2, h2_t).then_inc(used[s % 2], 1)
                    pe.wait_ge(s_pq, i * 4 + (s + 1))
                    pe.wait_ge(s_top, i * 4 + (1 + max(s - 1, 0)))
                    pe.wait_ge(s_late, i * 4 + (1 + max(s - 1, 0)))
                    for b in range(BLOCKS):
                        for c in range(2):
                            last = mm(ps[:, 2 + 2 * b + s % 2, c * P:(c + 1) * P],
                                      pq_t[s % 2][:, c * TOKENS + b * P:c * TOKENS + (b + 1) * P],
                                      sk[:, ds((i * 4 + s) * 2 + c, 1), :].rearrange("p a n -> p (a n)"), start=True, stop=True)
                    last.then_inc(s_ks, 1)

            def weigh_rows(b, heads, first=False, skip=()):
                rows = [e for e in range(TOPK) if e not in skip]
                for n_row, e in enumerate(rows):
                    s = e % V_RING
                    pe.wait_ge(s_dg, heads * TOPK + (n_row + 1))
                    pe.wait_ge(v_loaded[s], heads * (16 * TOPK // V_RING) + (e // V_RING + 1) * 16)
                    for n in range(4):
                        last = mm(ps[:, 4 * b + n, :], diag[:, s], v_slot[s][:, n * 512:(n + 1) * 512],
                                  start=first and e == 0, stop=False, skip_group_check=True)
                        if skip and e == rows[-1] and n == 1:
                            last.then_inc(s_half, 1)
                    last.then_inc(v_used[s], 1)

            pe.wait_ge(s_top, 1 + HEADS)
            pe.wait_ge(s_late, 1 + HEADS)
            for b in range(BLOCKS):
                weigh_rows(b, b * HEADS, first=True)
                with pe.Fori(0, HEADS - 1 - b) as i:
                    weigh_rows(b, i + (b * HEADS + 1))
            weigh_rows(1, 2 * HEADS - 1, skip=VECTOR_ROWS)

        @block.vector
        def _(dve):
            me = Steps(dve, dve_step)
            v = nc.vector
            v.memset(buf_b[:], 0.0).then_inc(s_cleared, 1)
            v.memset(rms_eps, RMS_EPS).then_inc(s_cleared, 1)
            dve.wait_ge(s_cols, 48)
            me.link(v.tensor_tensor(lb_max, logits[:, 0], logits[:, 1], ALU.max))
            me.step(v.tensor_tensor(logits[:, 0], logits[:, 0], lb_max, ALU.subtract))
            v.tensor_tensor(logits[:, 1], logits[:, 1], lb_max, ALU.subtract).then_inc(s_cond, 1)
            dve.wait_ge(s_sig, 1)
            me.link(v.tensor_scalar(cond_sig, cond_sig, 1.0, None, ALU.add))
            me.link(v.reciprocal(cond_sig, cond_sig))
            me.link(v.tensor_tensor(cond, cond_in, cond_sig, ALU.mult))
            dve.wait_ge(s_sig, 2)
            me.link(v.tensor_tensor(lb_sum, logits[:, 0], logits[:, 1], ALU.add))
            me.link(v.reciprocal(lb_sum, lb_sum))
            me.link(v.tensor_tensor(lb, logits[:, 0], lb_sum, ALU.mult))
            me.link(v.tensor_scalar(lb_rest, lb, -1.0, 1.0, ALU.mult, ALU.add))

            def ada_tile(s, sums, k, turn):
                dve.wait_ge(ada_loaded[s], turn * 16 + 16)
                dve.wait_ge(ada_used[1 - s], turn + (1 + s))
                v.scalar_tensor_tensor(out=sums, in0=ada_slot[s], scalar=cond[:, ds(k, 1)], in1=sums,
                                       op0=ALU.mult, op1=ALU.add).then_inc(ada_used[s], 1)

            dve.wait_ge(s_bias[0], 16)
            with dve.Fori(0, 4) as i:
                for s in range(4):
                    dve.wait_ge(loaded[s], i * 16 + 16)
                    dve.wait_ge(used[s - 1], i + (1 + (s > 0)))
                    v.scalar_tensor_tensor(out=buf_b[:], in0=arena[:, s * CHUNK:(s + 1) * CHUNK], scalar=cond[:, ds(i * 4 + s, 1)],
                                           in1=buf_b[:], op0=ALU.mult, op1=ALU.add).then_inc(used[s], 1)
            dve.wait_ge(s_mod, 1)
            me.step(v.tensor_copy(shift1, ps[:, 0, 0:KT]))
            v.tensor_scalar(scale1, ps[:, 0, KT:2 * KT], 1.0, None, ALU.add).then_inc(s_modc, 1)
            dve.wait_ge(s_modc, 1)
            dve.wait_ge(s_x, 16)
            for k in range(KT // 2):
                v.tensor_scalar(h_t[:, k], h_t[:, k], scale1[:, k:k + 1], shift1[:, k:k + 1], ALU.mult, ALU.add).then_inc(s_h, 1)

            dve.wait_ge(s_bias[1], 16)
            sums = mod_rows[:, 0:ADA_COLS]
            with me.loop(PAIRS, 2) as i:
                for r in range(2):
                    ada_tile(r, sums, i * 4 + r, i * 2)
                dve.wait_ge(used[1], i + (1 + F_ATTN[1] + 1))
                v.tensor_copy(k_t, ps[:, 1, :].rearrange("p (h t) -> p h t", h=2)).then_inc(s_k, 1)
                dve.wait_ge(s_log, i + 1)
                z = ps[:, 3:5, 0:384]
                me.link(v.scalar_tensor_tensor(out=a_exp, in0=z, scalar=0.0, in1=a_log, op0=ALU.max, op1=ALU.add))
                for h in range(2):
                    last = v.scalar_tensor_tensor(out=a_pen[:, h], in0=a_exp[:, h], scalar=-1.0, in1=before, op0=ALU.mult, op1=ALU.mult)
                last.then_inc(s_pen, 1)
                me.link(v.tensor_tensor(a_w, z, a_exp, ALU.subtract))
                dve.wait_ge(s_tail, i + 1)
                v.tensor_tensor(a_w, ps[:, 5:7, 0:384], a_w, ALU.add).then_inc(s_u, 1)
                dve.wait_ge(s_wexp, i + 1)
                for h in range(2):
                    last = v.tensor_tensor(a_w[:, h], a_w[:, h], before, ALU.mult)
                last.then_inc(s_w, 1)
                for r in range(2):
                    ada_tile(r, sums, i * 4 + (r + 2), i * 2 + 1)

            sums = mod_rows[:, ADA_COLS:2 * ADA_COLS]
            with me.loop(PAIRS, 9) as i:
                dve.wait_ge(s_ef, i + 1)
                me.link(v.tensor_scalar(f_gate, f_gate, 1.0, None, ALU.add))
                me.link(v.reciprocal(f_gate, f_gate))
                for h in range(2):
                    v.tensor_scalar(f_gate[:, h * 256:(h + 1) * 256], f_gate[:, h * 256:(h + 1) * 256],
                                    lb_rest[:, ds(i * 2 + h, 1)], lb[:, ds(i * 2 + h, 1)], ALU.mult, ALU.add).then_inc(s_f, 1)
                dve.wait_ge(s_f, i * 2 + 2)
                me.step(v.tensor_scalar(f_key, f_gate, -1.0, 1.0, ALU.mult, ALU.add))
                dve.wait_ge(s_lf, i + 1)
                for m in range(4):
                    me.step(v.tensor_tensor_scan(f_cum[:, m * P:(m + 1) * P], ones, f_log[:, m * P:(m + 1) * P], 0.0, ALU.mult, ALU.add))
                me.settle()
                cum = f_cum.rearrange("p (h b t) -> p h b t", h=2, b=2)
                far = decay[:, 0].rearrange("p (h b) t -> p h b t", h=2)
                for h in range(2):
                    end = cum[:, h, 0, P - 1:P]
                    v.tensor_scalar(far[:, h, 0], cum[:, h, 0], -1.0, end, ALU.mult, ALU.add)
                    v.tensor_copy(far[:, h, 1], cum[:, h, 1])
                for n in range(LEVELS):
                    half = 1 << n
                    c = f_cum.rearrange("p (g a t) -> p g a t", a=2, t=half)
                    d = decay[:, n + 1].rearrange("p m t -> p (m t)").rearrange("p (g a t) -> p g a t", a=2, t=half)
                    end = c[:, :, 0, half - 1:half].to_broadcast([P, 256 // half, half])
                    v.tensor_tensor(d[:, :, 0], end, c[:, :, 0], ALU.subtract)
                    last = v.tensor_tensor(d[:, :, 1], c[:, :, 1], end, ALU.subtract)
                last.then_inc(s_d, 1)
                for r in range(2):
                    ada_tile(r, sums, i * 4 + r, i * 2 + KT // 2)
                dve.wait_ge(s_x2, i * 2 + 2)
                dve.wait_ge(s_hq, i + 1)
                key, query = (x.rearrange("p (h b t) -> p h b t", h=2, b=2) for x in (f_key, hq_t))
                v.tensor_tensor(far[:, :, 0], far[:, :, 0], key[:, :, 0], ALU.mult)
                v.tensor_tensor(far[:, :, 1], far[:, :, 1], query[:, :, 1], ALU.mult)
                for n in range(LEVELS):
                    half = 1 << n
                    d = decay[:, n + 1].rearrange("p m t -> p (m t)").rearrange("p (g a t) -> p g a t", a=2, t=half)
                    key, query = (x.rearrange("p (g a t) -> p g a t", a=2, t=half) for x in (f_key, hq_t))
                    v.tensor_tensor(d[:, :, 0], d[:, :, 0], key[:, :, 0], ALU.mult)
                    last = v.tensor_tensor(d[:, :, 1], d[:, :, 1], query[:, :, 1], ALU.mult)
                last.then_inc(s_x3, 1)
                for m in range(4):
                    dve.wait_ge(s_lv, i * 4 + (m + 1))
                    dve.wait_ge(s_sc, i * 4 + (m + 1))
                    bank = LEVEL_BANKS[m]
                    v.tensor_tensor(masked.rearrange("p l t -> p (l t)"), ps[:, bank:bank + 2, :].rearrange("p a n -> p (a n)"),
                                    level_mask, ALU.mult).then_inc(s_lvr, 1)
                    dve.wait_ge(s_lvr, i * 4 + (m + 1))
                    v.tensor_reduce(score_t[:, m], masked.rearrange("p l t -> p t l"), AX_X, ALU.add).then_inc(s_sc, 1)
                for r in range(2):
                    ada_tile(r, sums, i * 4 + (r + 2), i * 2 + (KT // 2 + 1))
                dve.wait_ge(s_rs, i + 1)
                for m in range(4):
                    last = v.tensor_scalar(o_norm[:, m], ps[:, 5, m * P:(m + 1) * P], rstd[:, m:m + 1], None, ALU.mult)
                last.then_inc(s_on, 1)
                dve.wait_ge(s_eg, i + 1)
                me.link(v.tensor_scalar(g_exp, g_exp, 1.0, None, ALU.add))
                me.link(v.reciprocal(g_exp, g_exp))
                for h in range(2):
                    w = slice(h * 256, (h + 1) * 256)
                    last = v.scalar_tensor_tensor(out=g_t[:, w], in0=ps[:, 7, w], scalar=norm_col[:, ds(i * 2 + h, 1)],
                                                  in1=g_exp[:, w], op0=ALU.mult, op1=ALU.mult)
                last.then_inc(s_g, 1)
                dve.wait_ge(s_tr, i + 1)
                dve.wait_ge(s_g, i + 2)
                v.tensor_tensor(hgrn_t[:, ds(i * 2, 2), :], ps[:, 6, :].rearrange("p (h t) -> p h t", h=2),
                                g_t.rearrange("p (h t) -> p h t", h=2), ALU.mult).then_inc(s_bt, 1)

            with me.loop(GATES, 4) as i:
                dve.wait_ge(s_ea, i + 2)
                me.link(v.tensor_scalar(ga_exp, ga_exp, 1.0, None, ALU.add))
                me.link(v.reciprocal(ga_exp, ga_exp))
                dve.wait_ge(s_eb, i + 2)
                me.link(v.tensor_scalar(gb_exp, gb_exp, 1.0, None, ALU.add))
                me.link(v.reciprocal(gb_exp, gb_exp))
                dve.wait_ge(s_a, i + 1)
                dve.wait_ge(s_mg, 1 + i)
                v.tensor_tensor(m_a, ps[:, 2, :], ga_exp, ALU.mult).then_inc(s_am, 1)
                dve.wait_ge(used[2], i + (1 + F_GATE[2] + 1))
                v.tensor_tensor(m_b, ps[:, 3, :], gb_exp, ALU.mult).then_inc(s_bm, 1)
                dve.wait_ge(s_am, i + 2)
                dve.wait_ge(s_bm, i + 2)
                v.tensor_tensor(merged_t[:, ds(i * 2, 2), :], m_a.rearrange("p (h t) -> p h t", h=2),
                                m_b.rearrange("p (h t) -> p h t", h=2), ALU.add).then_inc(s_mg, 1)

            dve.wait_ge(s_row, 1 + 16)
            dve.wait_ge(s_ln[0], 16)
            spare = pq_t[1]
            for n in range(4):
                c = slice(n * 512, (n + 1) * 512)
                me.link(v.scalar_tensor_tensor(out=spare, in0=scale2[:, c], scalar=1.0, in1=ln_slot[0][:, 1, c], op0=ALU.add, op1=ALU.mult))
                me.link(v.tensor_tensor(shift2[:, c], shift2[:, c], spare, ALU.add))
            me.link(v.scalar_tensor_tensor(out=scale2, in0=scale2, scalar=1.0, in1=ln_slot[0][:, 0], op0=ALU.add, op1=ALU.mult))
            gain2, bias2 = scale2, shift2

            dve.wait_ge(s_xr, 16)
            y = out_term
            with me.loop(2, 8) as i:
                for s in range(4):
                    dve.wait_ge(used[s], i + (1 + F_OUT[s] + 1))
                    dve.wait_ge(s_y, i * 4 + (1 + s))
                    c = ds((i * 4 + s) * COLS, COLS)
                    g = mod_rows[:, ds((i * 4 + s) * COLS, COLS)]
                    for b in range(BLOCKS):
                        last = v.scalar_tensor_tensor(out=y[:, b], in0=g, scalar=1.0, in1=ps[:, s, b * COLS:(b + 1) * COLS],
                                                      op0=ALU.add, op1=ALU.mult)
                    me.link(last)
                    v.scalar_tensor_tensor(out=xr[:, :, c], in0=xr[:, :, c], scalar=ALPHA, in1=y, op0=ALU.mult, op1=ALU.add)\
                        .then_inc(s_y, 1)
                    if s % 2:
                        dve.wait_ge(s_y, i * 4 + (2 + s))
                        for b in range(BLOCKS):
                            me.step(v.bn_stats(ln_stats[b][:, ds(i * 2 + s // 2, 1)].rearrange("p a c -> p (a c)"),
                                               xr[:, b, ds((i * 4 + (s - 1)) * COLS, 512)]))
            me.settle()

            def mean_and_variance(b):
                me.link(v.bn_aggr(ln_mv[b], ln_stats[b].rearrange("p a c -> p (a c)")))
                v.tensor_scalar(ln_mv[b][:, 1:2], ln_mv[b][:, 1:2], LN_EPS, None, ALU.add).then_inc(s_var, 1)

            def ln_statistics(rows, b):
                for q in range(4):
                    me.step(v.bn_stats(ln_stats[b][:, q], rows[:, q * 512:(q + 1) * 512]))
                me.settle()
                mean_and_variance(b)

            for b in range(BLOCKS):
                mean_and_variance(b)
            for b in range(BLOCKS):
                v.scalar_tensor_tensor(out=h2[:, b], in0=xr[:, b], scalar=ln_mv[b][:, 0:1], in1=gain2,
                                       op0=ALU.subtract, op1=ALU.mult).then_inc(s_cen, 1)
                dve.wait_ge(s_cen, b + 1)
                dve.wait_ge(s_std, b + 1)
                v.scalar_tensor_tensor(out=h2[:, b], in0=h2[:, b], scalar=ln_rstd[b], in1=bias2,
                                       op0=ALU.mult, op1=ALU.add).then_inc(s_h2, 1)
            for b in range(BLOCKS):
                dve.wait_ge(s_xn, b + 1)
                me.link(v.tensor_tensor(xr[:, b], xr[:, b], ln_slot[0][:, 0], ALU.mult))
                me.link(v.tensor_tensor(xr[:, b], xr[:, b], ln_slot[0][:, 1], ALU.add))

            def spread(a, n):
                return a.unsqueeze(2).to_broadcast([P, n, TOPK])

            def top16(values, indices, source, reduced, first_wait):
                n = range(len(source))
                wait_alone(dve, *first_wait)
                for j in n:
                    me.step(v.max(values[j][:, 0:8], source[j]))
                wait_alone(dve, *me.reached())
                for j in n:
                    me.step(v.max_index(indices[j][:, 0:8], values[j][:, 0:8], source[j]))
                    me.step(v.match_replace(reduced[j], values[j][:, 0:8], source[j], LOWEST))
                wait_alone(dve, *me.reached())
                for j in n:
                    me.step(v.max(values[j][:, 8:16], reduced[j]))
                wait_alone(dve, *me.reached())
                for j in n:
                    last = v.max_index(indices[j][:, 8:16], values[j][:, 8:16], reduced[j])
                    if j < n[-1]:
                        me.step(last)
                return last

            def choose_experts(b, h, n, source, source_ready, signal):
                top16([top_v[:, c] for c in range(2)], [top_i[:, c] for c in range(2)], source,
                      [rest[:, c] for c in range(2)], source_ready).then_inc(signal[0], 1)
                dve.wait_ge(*signal)
                me.step(v.tensor_copy(top_if, top_i[:]))
                me.step(v.tensor_tensor(cand, spread(top_v[:, 0], TOPK), top_v[:, 1].unsqueeze(1).to_broadcast([P, TOPK, TOPK]), ALU.add))
                me.link(top16([best], [pos[:]], [cand.rearrange("p a c -> p (a c)")], [onehot[:, 0:256]], me.reached()))
                v.tensor_scalar(soft, best, best[:, 0:1], None, ALU.subtract).then_inc(s_sd, 1)
                me.step(v.tensor_scalar(hilo[:, 0], pos[:], 4, None, ALU.logical_shift_right))
                me.link(v.tensor_scalar(hilo[:, 1], pos[:], 15, None, ALU.bitwise_and))
                me.link(v.tensor_copy(hilo_f, hilo[:].rearrange("p c k -> p (c k)")))
                me.link(v.tensor_tensor(onehot.rearrange("p (k a) -> p k a", a=TOPK), spread(hilo_f, 2 * TOPK),
                                        iota.unsqueeze(1).to_broadcast([P, 2 * TOPK, TOPK]), ALU.is_equal))
                for c in range(2):
                    half = onehot[:, c * 256:(c + 1) * 256].rearrange("p (k a) -> p k a", a=TOPK)
                    me.step(v.tensor_tensor(half, half, top_if[:, c].unsqueeze(1).to_broadcast([P, TOPK, TOPK]), ALU.mult))
                me.settle()
                me.link(v.tensor_reduce(expert_f, onehot.rearrange("p (k a) -> p k a", a=TOPK), AX_X, ALU.add))
                me.link(v.scalar_tensor_tensor(out=expert_f[:, 0:TOPK], in0=expert_f[:, 0:TOPK], scalar=float(N_KEYS),
                                               in1=expert_f[:, TOPK:], op0=ALU.mult, op1=ALU.add))
                v.tensor_copy(expert[:, b, ds(h * TOPK, TOPK)], expert_f[:, 0:TOPK]).then_inc(s_ex, 1)
                dve.wait_ge(s_se, n + 1)
                me.link(v.tensor_reduce(soft_sum, soft, AX_X, ALU.add))
                me.link(v.reciprocal(soft_sum, soft_sum))
                v.tensor_scalar(gates[:, b, ds(h * TOPK, TOPK)], soft, soft_sum, None, ALU.mult).then_inc(s_gt, 1)

            def choose_late(h):
                me.link(v.tensor_copy(late, late_scores[:, ds(h * 2, 2), :]))
                choose_experts(1, h, h + HEADS, [late[:, c] for c in range(2)], me.reached(), (s_read, h + 1))

            def reduce_rows(b, heads, which, turn=0, sums=act):
                for e in which:
                    s = e % U_RING
                    dve.wait_ge(u_loaded[s], heads * (16 * TOPK // U_RING) + (e // U_RING + 1) * 16 + turn * 16)
                    v.tensor_tensor_reduce(out=u_slot[s], in0=u_slot[s], in1=h2[:, b], scale=1.0, scalar=0.0,
                                           op0=ALU.mult, op1=ALU.add, accum_out=sums[:, e:e + 1]).then_inc(u_used[s], 1)

            def weigh(b, h, heads):
                dve.wait_ge(s_gel, heads + 1)
                v.tensor_tensor(wgt, gel, gates[:, b, ds(h * TOPK, TOPK)], ALU.mult).then_inc(s_wgt, 1)

            def merge_block0():
                for s in range(V_RING):
                    dve.wait_ge(v_used[s], 1 + SLOTS // V_RING)
                rows = h2[:, 0]
                me.link(v.scalar_tensor_tensor(out=rows, in0=gate2, scalar=1.0, in1=ps[:, 0:4, :].rearrange("p a n -> p (a n)"),
                                               op0=ALU.add, op1=ALU.mult))
                me.link(v.scalar_tensor_tensor(out=rows, in0=xr[:, 0], scalar=ALPHA, in1=rows, op0=ALU.mult, op1=ALU.add))

            def merge_block1():
                dve.wait_ge(s_wgt, BLOCKS * HEADS)
                for s in range(U_RING):
                    dve.wait_ge(u_used[s], 1 + BLOCKS * SLOTS // U_RING)
                part = u_slot[0]
                for e in VECTOR_ROWS:
                    s = e % V_RING
                    dve.wait_ge(v_loaded[s], BLOCKS * SLOTS // V_RING * 16)
                    if e == VECTOR_ROWS[0]:
                        row = v.tensor_scalar(part, v_slot[s], wgt[:, e:e + 1], None, ALU.mult)
                    else:
                        row = v.scalar_tensor_tensor(out=part, in0=v_slot[s], scalar=wgt[:, e:e + 1], in1=part, op0=ALU.mult, op1=ALU.add)
                    row.then_inc(v_used[s], 1)
                    dve.wait_ge(v_used[s], 1 + BLOCKS * SLOTS // V_RING)
                me.link(v.scalar_tensor_tensor(out=part, in0=gate2, scalar=1.0, in1=part, op0=ALU.add, op1=ALU.mult))
                me.link(v.scalar_tensor_tensor(out=part, in0=xr[:, 1], scalar=ALPHA, in1=part, op0=ALU.mult, op1=ALU.add))
                rows = h2[:, 1]
                dve.wait_ge(s_half, 1)
                for j, c in enumerate(halves):
                    if j:
                        for s in range(V_RING):
                            dve.wait_ge(v_used[s], 1 + BLOCKS * SLOTS // V_RING)
                    me.step(v.scalar_tensor_tensor(out=rows[:, c], in0=gate2[:, c], scalar=1.0,
                                                   in1=ps[:, 4 + 2 * j:6 + 2 * j, :].rearrange("p a n -> p (a n)"),
                                                   op0=ALU.add, op1=ALU.mult))
                me.settle()
                me.link(v.tensor_tensor(rows, rows, part, ALU.add))

            def finish_rows(b, n):
                rows = h2[:, b]
                ln_statistics(rows, b)
                dve.wait_ge(s_ln[1], 16)
                for c in halves:
                    me.step(v.scalar_tensor_tensor(out=rows[:, c], in0=rows[:, c], scalar=ln_mv[b][:, 0:1], in1=ln_slot[1][:, 0, c],
                                                   op0=ALU.subtract, op1=ALU.mult))
                me.settle()
                dve.wait_ge(s_std, n)
                for c in halves:
                    v.scalar_tensor_tensor(out=rows[:, c], in0=rows[:, c], scalar=ln_rstd[b], in1=ln_slot[1][:, 1, c],
                                           op0=ALU.mult, op1=ALU.add).then_inc(s_fin, 1)

            with me.loop(4, 2 * STEPS_OF_CHOICE) as i:
                for s in range(2):
                    choose_experts(0, i * 2 + s, i * 2 + s, [ps[:, 2 + s, c * P:(c + 1) * P] for c in range(2)],
                                   (s_ks, i * 2 + (s + 1)), (s_top, i * 2 + (s + 2)))
                reduce_rows(0, 0, range(U_RING), turn=i, sums=first_act)
                dve.wait_ge(u_used[U_RING - 1], i + 2)
                v.tensor_copy(act[:, ds(i * U_RING, U_RING)], first_act).then_inc(s_first, 1)
                dve.wait_ge(s_first, i + 1)
            weigh(0, 0, 0)
            reduce_rows(0, 1, range(U_RING))
            choose_late(0)
            reduce_rows(0, 1, range(U_RING, TOPK))
            weigh(0, 1, 1)
            with me.loop(HEADS - 2, STEPS_OF_CHOICE + 1) as i:
                choose_late(i + 1)
                reduce_rows(0, i + 2, range(TOPK))
                weigh(0, i + 2, i + 2)
            choose_late(HEADS - 1)
            reduce_rows(1, HEADS, range(TOPK))
            weigh(1, 0, HEADS)
            merge_block0()
            finish_rows(0, BLOCKS + 1)
            with me.loop(HEADS - 1, 0) as i:
                reduce_rows(1, i + (HEADS + 1), range(TOPK))
                weigh(1, i + 1, i + (HEADS + 1))
            merge_block1()
            finish_rows(1, BLOCKS + 2)


def kernel(x, c, w_ada, b_ada, w_in, hg_lb_logits, hg_norm_g, w_branch_a, w_branch_b, w_out,
           ln1_g, ln1_b, peer_wq, peer_subkeys, peer_u, peer_v, ln2_g, ln2_b):
    import concourse.bacc as bacc
    from concourse.bass_utils import run_bass_kernel_spmd

    def f32(a):
        return np.asarray(a)

    def chunked(w):
        rows, n = w.shape
        return w.reshape(rows // P, P, n // COLS, COLS).transpose(2, 1, 0, 3).reshape(n // COLS, P, rows // P * COLS)

    w = chunked(f32(w_in)[0])
    sb_q, sb_k, sb_v, hg_q, hg_f, hg_i, hg_g = (w[n * PAIRS:(n + 1) * PAIRS] for n in range(7))
    gate_a, gate_b = w[7 * PAIRS:7 * PAIRS + GATES], w[7 * PAIRS + GATES:]
    branches = np.concatenate([chunked(f32(w_branch_a)[0]), chunked(f32(w_branch_b)[0])], axis=2)

    def woven(*roles):
        return np.stack(roles, axis=1).reshape(-1, P, CHUNK)

    weights = np.concatenate([woven(sb_q, sb_k, sb_v), woven(hg_f, hg_q, hg_i, hg_g), woven(gate_a, gate_b, branches),
                              chunked(f32(w_out)[0]), chunked(f32(peer_wq)[0])])
    x = f32(x)[0]
    arrays = {
        "consts": constants(),
        "x_rows": x.reshape(BLOCKS, P, D_MODEL).transpose(1, 0, 2),
        "x_t": x.reshape(TOKENS, KT, P).transpose(2, 1, 0).reshape(P, CHUNK),
        "cond_cols": f32(c)[0].reshape(KT, P).T,
        "ada": f32(w_ada)[0],
        "ada_bias": f32(b_ada),
        "weights": weights.reshape(N_CHUNKS * P, CHUNK),
        "lb_logits": f32(hg_lb_logits).reshape(2, HEADS, HEAD_DIM).transpose(2, 0, 1),
        "norm_gain": f32(hg_norm_g)[0].reshape(HEADS, HEAD_DIM).T,
        "ln_rows": np.stack([f32(a)[0] for a in (ln1_g, ln1_b, ln2_g, ln2_b)]),
        "subkeys_t": f32(peer_subkeys)[0].reshape(2 * HEADS, N_KEYS, P).transpose(2, 0, 1),
        "expert_u": f32(peer_u)[0],
        "expert_v": f32(peer_v)[0],
    }
    nc = bacc.Bacc("TRN2", target_bir_lowering=False, num_devices=1)
    arrays = {n: np.ascontiguousarray(a) for n, a in arrays.items()}
    args = [nc.dram_tensor(n, a.shape, F32, kind="ExternalInput").ap() for n, a in arrays.items()]
    out = nc.dram_tensor("out", (TOKENS, D_MODEL), F32, kind="ExternalOutput").ap()
    block_kernel(nc, *args, out)
    r = run_bass_kernel_spmd(nc, [arrays], core_ids=[0])
    return r.results[0]["out"].reshape(1, TOKENS, D_MODEL)
```
